# Optimizing a Trainium2 kernel written in Bass

```python
import jax, jax.numpy as jnp
from jax import lax
import numpy as np

D_MODEL = 1024
BATCH = 1
SEQ = 512
DEPTH = 1

CHUNK = 64
N_FOX_HEADS = 8
N_SB_HEADS = 8
HEAD_DIM = D_MODEL // (N_FOX_HEADS + N_SB_HEADS)
FOX_WIDTH = N_FOX_HEADS * HEAD_DIM
SB_WIDTH = N_SB_HEADS * HEAD_DIM
MIX_WIDTH = FOX_WIDTH + SB_WIDTH
PROJ_DIM = 3 * FOX_WIDTH + N_FOX_HEADS + 3 * SB_WIDTH
Q_BLOCK = 128
N_EXPERTS = 32
TOP_K = 4
D_FF = D_MODEL
SWIGLU_LIMIT = 7.0
SWIGLU_ALPHA = 1.702
MOE_BLOCK = 128
RMS_EPS = 1e-5

kernel_name = "hymba_fox_stickbreaking_moe_block"

def _rmsnorm(x, g):
    xf = x.astype(jnp.float32)
    y = xf * lax.rsqrt(jnp.mean(xf * xf, axis=-1, keepdims=True) + RMS_EPS)
    return (y * g.astype(jnp.float32)).astype(x.dtype)

def _to_heads(t, n_heads):
    b, s, _ = t.shape
    return t.reshape(b, s, n_heads, HEAD_DIM).transpose(0, 2, 1, 3).astype(jnp.float32)

def _from_heads(t):
    b, h, s, d = t.shape
    return t.transpose(0, 2, 1, 3).reshape(b, s, h * d)

def _forgetting_attention(q, k, v, c):
    seq = q.shape[2]
    scale = HEAD_DIM ** -0.5
    outs = []
    for i in range(seq // Q_BLOCK):
        q0, q1 = i * Q_BLOCK, (i + 1) * Q_BLOCK
        s = jnp.einsum('bhqd,bhkd->bhqk', q[:, :, q0:q1], k[:, :, :q1]) * scale
        s = s + c[:, :, q0:q1, None] - c[:, :, None, :q1]
        causal = jnp.arange(q0, q1)[:, None] >= jnp.arange(q1)[None, :]
        p = jax.nn.softmax(jnp.where(causal, s, -jnp.inf), axis=-1)
        outs.append(jnp.einsum('bhqk,bhkd->bhqd', p, v[:, :, :q1]))
    return jnp.concatenate(outs, axis=2)

def _stick_breaking_attention(q, k, v):
    seq = q.shape[2]
    scale = HEAD_DIM ** -0.5
    outs = []
    for i in range(seq // Q_BLOCK):
        q0, q1 = i * Q_BLOCK, (i + 1) * Q_BLOCK
        z = jnp.einsum('bhqd,bhkd->bhqk', q[:, :, q0:q1], k[:, :, :q1]) * scale
        strict = jnp.arange(q0, q1)[:, None] > jnp.arange(q1)[None, :]
        log_1mb = jnp.where(strict, jax.nn.log_sigmoid(-z), 0.0)
        suffix = lax.cumsum(log_1mb, axis=3, reverse=True) - log_1mb
        log_a = jnp.where(strict, jax.nn.log_sigmoid(z) + suffix, -jnp.inf)
        outs.append(jnp.einsum('bhqk,bhkd->bhqd', jnp.exp(log_a), v[:, :, :q1]))
    return jnp.concatenate(outs, axis=2)

def _moe(h, w_router, b_router, w1, b1, w2, b2):
    b, s, d = h.shape
    n_tok = b * s
    t = h.reshape(n_tok, d)
    logits = (t @ w_router + b_router).astype(jnp.float32)
    top_v, top_i = lax.top_k(logits, TOP_K)
    top_w = jax.nn.softmax(top_v, axis=-1)
    n_asg = n_tok * TOP_K
    flat_e = top_i.reshape(n_asg).astype(jnp.int32)
    flat_tok = jnp.arange(n_asg, dtype=jnp.int32) // TOP_K
    flat_w = top_w.reshape(n_asg)
    order = jnp.argsort(flat_e)
    se, stok, sw = flat_e[order], flat_tok[order], flat_w[order]
    counts = jnp.zeros((N_EXPERTS,), jnp.int32).at[flat_e].add(1)
    start = jnp.cumsum(counts) - counts
    padded = (counts + MOE_BLOCK - 1) // MOE_BLOCK * MOE_BLOCK
    pend = jnp.cumsum(padded)
    pstart = pend - padded
    dest = pstart[se] + jnp.arange(n_asg, dtype=jnp.int32) - start[se]
    n_blocks = -(-n_asg // MOE_BLOCK) + N_EXPERTS
    n_rows = n_blocks * MOE_BLOCK
    tok_pad = jnp.full((n_rows,), n_tok, jnp.int32).at[dest].set(stok)
    w_pad = jnp.zeros((n_rows,), jnp.float32).at[dest].set(sw)
    block_e = jnp.minimum(
        jnp.searchsorted(pend, jnp.arange(n_blocks, dtype=jnp.int32) * MOE_BLOCK, side='right'),
        N_EXPERTS - 1).astype(jnp.int32)
    t_pad = jnp.concatenate([t, jnp.zeros((1, d), t.dtype)], axis=0)
    xb = t_pad[tok_pad].reshape(n_blocks, MOE_BLOCK, d)

    def expert_rows(args):
        xe, e = args
        hh = xe @ w1[e] + b1[e]
        glu = jnp.minimum(hh[:, :D_FF], SWIGLU_LIMIT)
        lin = jnp.clip(hh[:, D_FF:], -SWIGLU_LIMIT, SWIGLU_LIMIT)
        act = glu * jax.nn.sigmoid(SWIGLU_ALPHA * glu) * (lin + 1.0)
        return act @ w2[e] + b2[e]

    yb = lax.map(expert_rows, (xb, block_e)).reshape(n_rows, d)
    out = jnp.zeros((n_tok + 1, d), jnp.float32).at[tok_pad].add(
        yb.astype(jnp.float32) * w_pad[:, None])
    return out[:n_tok].reshape(b, s, d).astype(h.dtype)

def setup_inputs(seed: int = 0) -> dict:
    key = jax.random.key(seed)
    ks = jax.random.split(key, 16)
    nrm = jax.random.normal
    L = DEPTH
    x = nrm(ks[0], (BATCH, SEQ, D_MODEL), jnp.float32)
    norm1_g = 1.0 + 0.02 * nrm(ks[1], (L, D_MODEL), jnp.float32)
    w_in = nrm(ks[2], (L, D_MODEL, PROJ_DIM), jnp.float32) * D_MODEL ** -0.5
    b_f = jnp.linspace(1.0, 5.0, N_FOX_HEADS, dtype=jnp.float32)[None, :] + 0.1 * nrm(ks[3], (L, N_FOX_HEADS), jnp.float32)
    g_fox = 1.0 + 0.02 * nrm(ks[4], (L, FOX_WIDTH), jnp.float32)
    g_sb = 1.0 + 0.02 * nrm(ks[5], (L, SB_WIDTH), jnp.float32)
    w_out = nrm(ks[6], (L, MIX_WIDTH, D_MODEL), jnp.float32) * MIX_WIDTH ** -0.5
    norm2_g = 1.0 + 0.02 * nrm(ks[7], (L, D_MODEL), jnp.float32)
    w_router = nrm(ks[8], (L, D_MODEL, N_EXPERTS), jnp.float32) * D_MODEL ** -0.5
    b_router = 0.01 * nrm(ks[9], (L, N_EXPERTS), jnp.float32)
    w1 = nrm(ks[10], (L, N_EXPERTS, D_MODEL, 2 * D_FF), jnp.float32) * D_MODEL ** -0.5
    b1 = 0.01 * nrm(ks[11], (L, N_EXPERTS, 2 * D_FF), jnp.float32)
    w2 = nrm(ks[12], (L, N_EXPERTS, D_FF, D_MODEL), jnp.float32) * D_FF ** -0.5
    b2 = 0.01 * nrm(ks[13], (L, N_EXPERTS, D_MODEL), jnp.float32)
    norm_f_g = 1.0 + 0.02 * nrm(ks[14], (D_MODEL,), jnp.float32)
    return {"x": x, "norm1_g": norm1_g, "w_in": w_in, "b_f": b_f, "g_fox": g_fox,
            "g_sb": g_sb, "w_out": w_out, "norm2_g": norm2_g, "w_router": w_router,
            "b_router": b_router, "w1": w1, "b1": b1, "w2": w2, "b2": b2,
            "norm_f_g": norm_f_g}

def reference(x, norm1_g, w_in, b_f, g_fox, g_sb, w_out, norm2_g, w_router,
              b_router, w1, b1, w2, b2, norm_f_g):
    b, s, _ = x.shape
    splits = [FOX_WIDTH, 2 * FOX_WIDTH, 3 * FOX_WIDTH, 3 * FOX_WIDTH + N_FOX_HEADS,
              3 * FOX_WIDTH + N_FOX_HEADS + SB_WIDTH,
              3 * FOX_WIDTH + N_FOX_HEADS + 2 * SB_WIDTH]
    for l in range(DEPTH):
        h = _rmsnorm(x, norm1_g[l])
        proj = h @ w_in[l]
        fq, fk, fv, f_logit, sq, sk, sv = jnp.split(proj, splits, axis=-1)
        log_f = jax.nn.log_sigmoid(f_logit.astype(jnp.float32) + b_f[l].astype(jnp.float32))
        c = jnp.cumsum(log_f, axis=1).transpose(0, 2, 1)
        fox = _forgetting_attention(_to_heads(fq, N_FOX_HEADS), _to_heads(fk, N_FOX_HEADS),
                                    _to_heads(fv, N_FOX_HEADS), c)
        sb = _stick_breaking_attention(_to_heads(sq, N_SB_HEADS), _to_heads(sk, N_SB_HEADS),
                                       _to_heads(sv, N_SB_HEADS))
        mix = jnp.concatenate([_rmsnorm(_from_heads(fox), g_fox[l]),
                               _rmsnorm(_from_heads(sb), g_sb[l])], axis=-1).astype(x.dtype)
        x = x + mix @ w_out[l]
        x = x + _moe(_rmsnorm(x, norm2_g[l]), w_router[l], b_router[l],
                     w1[l], b1[l], w2[l], b2[l])
    return _rmsnorm(x, norm_f_g)


_drawn_inputs = setup_inputs


def setup_inputs(seed=0):
    import zlib

    import numpy as np

    out = dict(_drawn_inputs(seed))
    spreads = {}
    factors = {'b1': 8.0, 'b2': 8.0, 'norm_f_g': 2.876}
    for name, (base, spread) in spreads.items():
        noise = np.random.default_rng([zlib.crc32(name.encode()), seed]).standard_normal(out[name].shape)
        drawn = base * np.exp(spread * noise) if base else spread * noise
        out[name] = __import__('jax').numpy.asarray(drawn.astype(out[name].dtype))
    for name, factor in factors.items():
        out[name] = (out[name] * factor).astype(out[name].dtype)
    return out
```

```python
import concourse.bass as bass
from concourse import mybir
from contextlib import ExitStack

F32 = mybir.dt.float32
F32R = mybir.dt.float32r
BF16 = mybir.dt.bfloat16
I32 = mybir.dt.int32
U32 = mybir.dt.uint32
ACT = mybir.ActivationFunctionType
ALU = mybir.AluOpType
AX = mybir.AxisListType

P = 128
D = 1024
KT = D // P
S = 512
TT = S // P
NH = 8
HD = 64
HW = NH * HD
E = 32
TOPK = 4
FF = D
EPS = 1e-5
LIMIT = 7.0
ALPHA = 1.702
MASKED = -1e30
BANK = 512
SLOT = 2048
SLOTS = 12
PIECE = 1024
STAGES = 4
UNITS = NH * TT
OVER = S * TOPK // P - 1
ITEMS = E + OVER
W_IN_PIECES = 2 * SLOTS
W_OUT_PIECES = KT
MOE0 = W_IN_PIECES + W_OUT_PIECES
OPROJ_PIECES = W_OUT_PIECES
W1P, W2P = 2 * KT, KT
EMPTY = 8192.0


def build(nc, x, norm1_g, w_in, b_f, g_fox, g_sb, w_out, norm2_g, w_router, b_router, w1, b1, w2, b2,
          norm_f_g, out):
    x_d, out_d = x[0], out[0]
    w_in_d, w_out_d, w_router_d = w_in[0], w_out[0], w_router[0]
    w1_d = w1[0].rearrange("e (k p) n -> e k p n", p=P)
    w2_d = w2[0].rearrange("e (k p) n -> e k p n", p=P)

    with ExitStack() as ctx:
        def sb(name, shape, dt=F32):
            return ctx.enter_context(nc.sbuf_tensor(name, shape, dt))

        def sem(name):
            return ctx.enter_context(nc.semaphore(name))

        tn_d = nc.dram_tensor("tn_scratch", (S, D), F32, kind="Internal").ap()
        x2_d = nc.dram_tensor("x2_scratch", (S, D), F32, kind="Internal").ap()
        y_d = nc.dram_tensor("y_scratch", (S * TOPK, D), F32, kind="Internal").ap()

        ring = sb("ring", [P, SLOTS * SLOT])
        stage_hi = sb("stage_hi", [P, STAGES, PIECE], F32R)
        stage_lo = sb("stage_lo", [P, STAGES, PIECE], F32R)
        act_hi = sb("act_hi", [P, KT * S], F32R)
        act_lo = sb("act_lo", [P, KT * S], F32R)
        qk = sb("qk", [P, 16, S])
        spbuf = sb("spbuf", [P, 2560])
        identF = sb("identF", [P, P])
        identB = sb("identB", [P, P], BF16)
        maskF = sb("maskF", [P, P], BF16)
        maskS = sb("maskS", [P, P], BF16)
        neg_tri = sb("neg_tri", [P, P])
        neg_one = sb("neg_one", [P, P])
        before = sb("before", [P, P])
        ones = sb("ones", [P, P])
        iotas = sb("iotas", [P, P])
        cols = sb("cols", [P, 96])
        gtab = sb("gtab", [P, ITEMS], I32)
        stab = sb("stab", [P, ITEMS], I32)
        wtab = sb("wtab", [P, ITEMS])
        seltab = sb("seltab", [64, ITEMS])
        eidtab = sb("eidtab", [1, 16], I32)
        novi = sb("novi", [1, 1], I32)
        gidx = sb("gidx", [P, 1], I32)
        sidx = sb("sidx", [P, 1], I32)
        wcol = sb("wcol", [P, 1])

        hT_hi = act_hi[:].rearrange("p (k t) -> p k t", k=KT)
        hT_lo = act_lo[:].rearrange("p (k t) -> p k t", k=KT)
        xT_hi = act_hi[:, 0:D].rearrange("p (k s) -> p k s", k=KT)
        xT_lo = act_lo[:, 0:D].rearrange("p (k s) -> p k s", k=KT)
        aT_hi = act_hi[:, D:2 * D].rearrange("p (k s) -> p k s", k=KT)
        aT_lo = act_lo[:, D:2 * D].rearrange("p (k s) -> p k s", k=KT)
        bias1 = act_hi[0:64, 2 * D:4 * D]
        bias2 = act_lo[0:64, 2 * D:3 * D]
        sel1 = act_lo[0:64, 3 * D:3 * D + P]
        sel2 = act_lo[0:64, 3 * D + P:3 * D + 2 * P]

        def slot(z):
            return ring[:, z * SLOT:(z + 1) * SLOT]

        qk2 = qk[:].rearrange("p (a b) t -> p a (b t)", b=2)
        xs = [qk2[:, 4 + i, :] for i in range(TT)]
        g1b = qk2[:, 0, :]
        sqjunk = qk2[:, 1, :]
        vbuf = ring[:, 0:2 * SLOT].rearrange("p (t d) -> p t d", t=TT)
        pbuf = slot(2)[:, 0:1024].rearrange("p (b n) -> p b n", b=2)
        ptbuf = slot(2)[:, 1024:2048].rearrange("p (b n) -> p b n", b=2)
        lbuf = slot(3)[:, 0:1024].rearrange("p (b n) -> p b n", b=2)
        abuf = slot(3)[:, 1024:2048].rearrange("p (b n) -> p b n", b=2)
        sel8 = slot(4)[0:NH, 0:NH * P].rearrange("p (h q) -> p h q", h=NH)
        negc = slot(4)[0:NH, 1024:1024 + S]
        csum = slot(4)[0:NH, 1536:1536 + S]
        x2 = [qk2[:, i, :] for i in (2, 3, 6, 7)]
        tn = [qk2[:, i, :] for i in (0, 1, 4, 5)]
        g2b = spbuf[:, 0:D]
        tT = spbuf[:, D:2 * D].rearrange("p (k t) -> p k t", k=KT)
        ohslot = spbuf[:, 0:2048].rearrange("p (a n) -> p a n", n=P)
        payload = qk[:, 8:11, :].rearrange("p a t -> p (a t)")[:, 0:16 * 2 * ITEMS].rearrange(
            "p (a c n) -> p a c n", a=16, c=2)
        gath = qk2[:, 0, :]
        glu = qk2[:, 1, :]
        lin = qk2[:, 2, :]
        sig = qk2[:, 3, :]
        yout = qk2[:, 4, :]
        gfb = qk2[:, 5, :]
        rt = slot(4)

        bank = [ctx.enter_context(nc.psum_tensor(f"bank{i}", [P, BANK], F32)) for i in range(8)]

        ss1, rs1, r1 = cols[:, 0:4], cols[:, 4:8], cols[:, 8:12]
        negmax, rsum, rinv = cols[:, 12:14], cols[:, 14:16], cols[:, 16:18]
        gmix = cols[:, 18:26]
        ssm, rsm, rm = cols[:, 26:34], cols[:, 34:42], cols[:, 42:50]
        ss2, rs2, r2 = cols[:, 50:54], cols[:, 54:58], cols[:, 58:62]
        pmod = cols[0:64, 62:63]
        bfc = cols[0:NH, 63:64]
        ss3, rs3, r3 = cols[:, 64:68], cols[:, 68:72], cols[:, 72:76]
        row1 = cols[:, 76:92]
        epsc = cols[:, 92:93]
        smax = cols[:, 93:95]
        wfraw = sb("wfraw", [P, KT, NH])
        wfr = sb("wfr", [P, 2, KT * NH], F32R)
        wrt = slot(3)[:, 0:KT * E].rearrange("p (k e) -> p k e", k=KT)
        brt = slot(3)[0:1, 512:512 + E]

        full = [sem(f"slot{z}_full") for z in range(SLOTS)]
        x_in, vec_in, wrt_in = sem("x_in"), sem("vec_in"), sem("wrt_in")
        g2_in, bias_in, gf_in = sem("g2_in"), sem("bias_in"), sem("gf_in")
        consts = sem("consts")
        split_hi, split_lo = sem("split_hi"), sem("split_lo")
        used = sem("pieces_used")
        h_sq, h_norm, h_turned, h_hi, h_lo = (sem(n) for n in ("h_sq", "h_norm", "h_turned", "h_hi", "h_lo"))
        qk_copied, v_copied = sem("qk_copied"), sem("v_copied")
        f_split, f_mm, f_steps, negc_ready = sem("f_split"), sem("f_mm"), sem("f_steps"), sem("negc_ready")
        s_ready, neg_ready, p_ready, ps_ready = sem("s_ready"), sem("neg_ready"), sem("p_ready"), sem("ps_ready")
        pt_turned, pt_ready, pvf_done = sem("pt_turned"), sem("pt_ready"), sem("pvf_done")
        z_ready, absz, ln_ready, sp_ready = sem("z_ready"), sem("absz"), sem("ln_ready"), sem("sp_ready")
        e_ready = sem("e_ready")
        loga_ready, a_ready, pvs_done = sem("loga_ready"), sem("a_ready"), sem("pvs_done")
        mix_hi, mix_sq, mix_lo = sem("mix_hi"), sem("mix_sq"), sem("mix_lo")
        ssm_done, rm_ready, oproj, x2_add = sem("ssm_done"), sem("rm_ready"), sem("oproj"), sem("x2_add")
        rsm_ready = sem("rsm_ready")
        x2_in, x2_sq, x2_rs, tn_ready = sem("x2_in"), sem("x2_sq"), sem("x2_rs"), sem("tn_ready")
        x2_out, tn_out = sem("x2_out"), sem("tn_out")
        tn_turned, tT_copied, logits_done, lg_copied = (sem(n) for n in ("tn_turned", "tT_copied", "logits_done", "lg_copied"))
        exp4, onehots, counted, slots_ready, tab_mm, tables = (sem(n) for n in ("exp4", "onehots", "counted", "slots_ready", "tab_mm", "tables"))
        bias_hi, bias_lo = sem("bias_hi"), sem("bias_lo")
        gath_zero = sem("gath_zero")
        idx_copied, gathered, x_turned, xT_hi_r, xT_lo_r = (sem(n) for n in ("idx_copied", "gathered", "x_turned", "xT_hi_ready", "xT_lo_ready"))
        sel1_r, sel2_r, sel1_used, clipped, sig_done, act_made = (sem(n) for n in ("sel1_ready", "sel2_ready", "bias1_added", "clipped", "sig_done", "act_made"))
        gs_made, weight_ready = sem("gs_made"), sem("weight_ready")
        a_turned, aT_hi_r, aT_lo_r, y_ready = (sem(n) for n in ("a_turned", "aT_hi_ready", "aT_lo_ready", "y_ready"))
        sidx_copied, scattered, all_scattered, yout_free = (sem(n) for n in ("sidx_copied", "scattered", "all_scattered", "yout_free"))
        fin_in, fin_sum, fin_sq, fin_rs, fin_ready, out_done = (sem(n) for n in ("fin_in", "fin_sum", "fin_sq", "fin_rs", "fin_ready", "out_done"))
        steps = {n: sem(n + "_steps") for n in ("pool", "act", "dve")}
        count = {n: 0 for n in steps}

        def wait(eng, semaphore, value):
            if not (isinstance(value, int) and value == 0):
                eng.wait_ge(semaphore, value)

        def link(eng, name, ins):
            count[name] += 1
            ins.then_inc(steps[name], 1)
            eng.wait_ge(steps[name], count[name])

        def piece_ap(g):
            if g < W_IN_PIECES:
                return ring[:, g * PIECE:(g + 1) * PIECE]
            h = g - W_IN_PIECES
            return ring[:, 5 * SLOT + h * PIECE:5 * SLOT + (h + 1) * PIECE]

        def moe_slot(c):
            return (c + 9) % SLOTS

        def loads_before(z):
            return 2 if 5 <= z < 9 else 1

        class Run:
            def __init__(self, first, n, base):
                self.first, self.n, self.base = first, n, base
                self.turn0 = (base - MOE0) // (2 * SLOTS)

        MAIN = Run(0, E, MOE0)
        REST = Run(E, OVER, MOE0 + E * (W1P + W2P))

        block = ctx.enter_context(nc.Block())

        @block.sync
        def _(sp):
            for t in range(TT):
                sp.dma_start(xs[t], x_d[t * P:(t + 1) * P, :]).then_inc(x_in, 16)
                if t == 0:
                    sp.dma_start(g1b, norm1_g[0:1, :].partition_broadcast(P)).then_inc(x_in, 16)
            for z in range(SLOTS):
                group, half = z // 2, z % 2
                c0 = group * HW + (NH if group >= 3 else 0)
                sp.dma_start(slot(z).rearrange("p (k n) -> p k n", k=4),
                             w_in_d.rearrange("(k p) n -> p k n", p=P)[:, 4 * half:4 * half + 4, c0:c0 + HW]
                             ).then_inc(full[z], 16)
            for z in range(5, 9):
                sp.wait_ge(split_lo, 2 * z + 2)
                sp.dma_start(slot(z).rearrange("p (k n) -> p k n", k=2),
                             w_out_d.rearrange("(k p) n -> p k n", p=P)[:, 2 * (z - 5):2 * (z - 5) + 2, :]
                             ).then_inc(full[z], 16)

            def load_w1(e, k, z):
                sp.dma_start(slot(z), w1_d[e, k]).then_inc(full[z], 16)

            for c in range(3):
                sp.wait_ge(split_lo, 2 * moe_slot(c) + 2)
                load_w1(0, c, moe_slot(c))
            sp.wait_ge(z_ready, UNITS)
            sp.wait_ge(s_ready, UNITS)
            sp.wait_ge(mix_sq, 2 * NH)
            for t in range(TT):
                sp.dma_start(x2[t], x_d[t * P:(t + 1) * P, :]).then_inc(x2_in, 16)
            sp.dma_start(g2b, norm2_g[0:1, :].partition_broadcast(P)).then_inc(g2_in, 16)
            sp.wait_ge(mix_hi, 2 * NH)
            sp.dma_start(wrt, w_router_d.rearrange("(k p) e -> p k e", p=P)).then_inc(wrt_in, 16)
            sp.dma_start(brt, b_router[0:1, :]).then_inc(wrt_in, 16)
            for c in range(3, 6):
                load_w1(0, c, moe_slot(c))
            for t in range(TT):
                sp.wait_ge(tn_ready, t + 1)
                sp.dma_start(tn_d[t * P:(t + 1) * P, :], tn[t]).then_inc(tn_out, 16)
                sp.dma_start(x2_d[t * P:(t + 1) * P, :], x2[t]).then_inc(x2_out, 16)
            for h in range(2):
                sp.wait_ge(split_lo, MOE0)
                sp.dma_start(slot(7)[32 * h:32 * h + 32, :], b1[0]).then_inc(bias_in, 16)
                sp.dma_start(slot(8)[32 * h:32 * h + 32, 0:D], b2[0]).then_inc(bias_in, 16)
            sp.wait_ge(logits_done, TT)
            load_w1(0, 6, moe_slot(6))
            sp.wait_ge(tables, 1)
            load_w1(0, 7, moe_slot(7))

            def load_body(e_w1, e_w2, c, waits):
                z = (c + 5) % SLOTS
                if waits is not None:
                    sp.wait_ge(split_lo, waits)
                if c < KT:
                    src = w1_d[e_w1, c] if isinstance(e_w1, int) else \
                        w1_d[bass.ds(e_w1, 1), c].rearrange("e p n -> p (e n)")
                    sp.dma_start(slot(z), src).then_inc(full[z], 16)
                else:
                    k = 2 * (c - KT)
                    src = w2_d[e_w2, k:k + 2].rearrange("k p n -> p k n") if isinstance(e_w2, int) else \
                        w2_d[bass.ds(e_w2, 1), k:k + 2].rearrange("e k p n -> p (e k) n")
                    sp.dma_start(slot(z).rearrange("p (k n) -> p k n", k=2), src).then_inc(full[z], 16)

            for c in range(SLOTS):
                if c == 2:
                    sp.wait_ge(bias_lo, 2)
                load_body(1, 0, c, MOE0 if c < 4 else MOE0 + 2 * (c - 4) + 2)
            with sp.Fori(2, E) as t:
                for c in range(SLOTS):
                    load_body(t, t - 1, c, t * 24 + (MOE0 - 30 + 2 * c))
            last = MOE0 + 24 * E - 8
            for c in range(KT, SLOTS):
                sp.wait_ge(split_lo, last + 2 * (c - KT) - 24 + 2)
                z = ((last - MOE0) // 2 + (c - KT) + 9) % SLOTS
                k = 2 * (c - KT)
                sp.dma_start(slot(z).rearrange("p (k n) -> p k n", k=2),
                             w2_d[E - 1, k:k + 2].rearrange("k p n -> p k n")).then_inc(full[z], 16)

            sp.wait_ge(tables, 1)
            n_over = sp.value_load(novi[0:1, 0:1], min_val=0, max_val=OVER)
            with sp.If(n_over > 0):
                def expert(i):
                    return sp.value_load(eidtab[0:1, bass.ds(i, 1)] if not isinstance(i, int) else
                                         eidtab[0:1, i:i + 1], min_val=0, max_val=E - 1)
                e0 = expert(0)
                b = REST.base
                for c in range(KT):
                    z = moe_slot(c)
                    sp.wait_ge(split_lo, b + 2 * c - 24 + 2)
                    sp.dma_start(slot(z), w1_d[bass.ds(e0, 1), c].rearrange("e p n -> p (e n)")).then_inc(full[z], 16)
                with sp.Fori(1, OVER) as t:
                    ew1, ew2 = expert(t), expert(t - 1)
                    for c in range(SLOTS):
                        load_body(ew1, ew2, c, t * 24 + (b - 8 + 2 * c - 24 + 2))
                el = expert(OVER - 1)
                for c in range(KT, SLOTS):
                    z = ((24 * OVER - 8) // 2 + (c - KT) + 9) % SLOTS
                    k = 2 * (c - KT)
                    sp.wait_ge(split_lo, b + 24 * OVER - 8 + 2 * (c - KT) - 24 + 2)
                    sp.dma_start(slot(z).rearrange("p (k n) -> p k n", k=2),
                                 w2_d[bass.ds(el, 1), k:k + 2].rearrange("e k p n -> p (e k) n")).then_inc(full[z], 16)

            sp.wait_ge(all_scattered, 1)
            sp.dma_start(gfb, norm_f_g.rearrange("(a d) -> a d", a=1).partition_broadcast(P)).then_inc(gf_in, 16)
            sp.wait_ge(x2_out, 16 * TT)
            for t in range(TT):
                o = t * 5 * D
                sp.dma_start(ring[:, o:o + D], x2_d[t * P:(t + 1) * P, :]).then_inc(fin_in, 16)
                sp.dma_start(ring[:, o + D:o + 5 * D],
                             y_d.rearrange("(t j) d -> t (j d)", j=TOPK)[t * P:(t + 1) * P, :]).then_inc(fin_in, 16)
            for t in range(TT):
                sp.wait_ge(fin_ready, t + 1)
                sp.dma_start(out_d[t * P:(t + 1) * P, :], ring[:, t * 5 * D:t * 5 * D + D]).then_inc(out_done, 16)
            sp.wait_ge(out_done, 16 * TT)
            sp.wait_ge(tn_out, 16 * TT)

        @block.gpsimd
        def _(pool):
            pool.dma_start(wfraw[:], w_in_d.rearrange("(k p) n -> p k n", p=P)[:, :, 3 * HW:3 * HW + NH]).then_inc(vec_in, 16)
            pool.dma_start(bfc, b_f.rearrange("a h -> h a"), allow_slow_non_contiguous=True).then_inc(vec_in, 16)
            pool.dma_start(gmix[:, 0:4], g_fox[0].rearrange("(c p) -> p c", p=P), allow_slow_non_contiguous=True).then_inc(vec_in, 16)
            pool.dma_start(gmix[:, 4:8], g_sb[0].rearrange("(c p) -> p c", p=P), allow_slow_non_contiguous=True).then_inc(vec_in, 16)

            def fill(ap, value):
                link(pool, "pool", nc.gpsimd.memset(ap, value))

            def choose(ap, pattern, op, fill_value, base, mult):
                return nc.gpsimd.affine_select(out=ap, in_=ap, pattern=pattern, compare_op=op, fill=fill_value,
                                               base=base, channel_multiplier=mult)
            made = [0]

            def constant(ins):
                made[0] += 1
                ins.then_inc(consts, 1)
                pool.wait_ge(consts, made[0])

            def count_up(ap, pattern, base, mult):
                return nc.gpsimd.iota(ap, pattern, base=base, channel_multiplier=mult,
                                      allow_small_or_imprecise_dtypes=True)
            fill(identF[:], 0.0)
            constant(choose(identF[:], [[-1, P]], ALU.not_equal, 1.0, 0, 1))
            constant(nc.gpsimd.memset(epsc, EPS))
            fill(identB[:], 0.0)
            constant(choose(identB[:], [[-1, P]], ALU.not_equal, 1.0, 0, 1))
            fill(maskF[:], 0.0)
            constant(choose(maskF[:], [[-1, P]], ALU.is_ge, MASKED, 0, 1))
            fill(maskS[:], 0.0)
            constant(choose(maskS[:], [[1, P]], ALU.is_gt, MASKED, 0, -1))
            fill(neg_tri[:], -1.0)
            constant(choose(neg_tri[:], [[-1, P]], ALU.is_ge, 0.0, 0, 1))
            constant(nc.gpsimd.memset(neg_one[:], -1.0))
            fill(before[:], 1.0)
            constant(choose(before[:], [[1, P]], ALU.is_gt, 0.0, 0, -1))
            constant(nc.gpsimd.memset(ones[:], 1.0))
            constant(count_up(iotas[:], [[1, P]], 0, 0))
            constant(count_up(cols[0:32, 62:63], [[0, 1]], 0, 1))
            constant(count_up(cols[32:64, 62:63], [[0, 1]], 0, 1))
            constant(count_up(row1, [[TOPK * P, TT], [1, TOPK]], 1, TOPK))
            pool.wait_ge(split_lo, 10)
            fill(sel8, 0.0)
            constant(choose(sel8, [[-1, NH], [0, P]], ALU.not_equal, 1.0, 0, 1))

            bound, zero = pool.alloc_register("bound"), pool.alloc_register("nought")
            pool.reg_mov(zero, 0)

            def gather(i):
                if not (isinstance(i, int) and i == 0):
                    pool.wait_ge(x_turned, i)
                nc.gpsimd.tensor_copy(gidx[:], gtab[:, i:i + 1] if isinstance(i, int) else gtab[:, bass.ds(i, 1)]
                                      ).then_inc(idx_copied, 1)
                pool.wait_ge(idx_copied, i + 1)
                pool.reg_add(bound, zero, S - 1)
                nc.gpsimd.indirect_dma_start(out=gath, out_offset=None, in_=tn_d[:, :],
                                             in_offset=bass.IndirectOffsetOnAxis(ap=gidx[:, 0:1], axis=0),
                                             bounds_check=bound, oob_is_err=False).then_inc(gathered, 16)

            def scatter(i):
                pool.wait_ge(y_ready, i + 1)
                nc.gpsimd.tensor_copy(sidx[:], stab[:, i:i + 1] if isinstance(i, int) else stab[:, bass.ds(i, 1)]
                                      ).then_inc(sidx_copied, 1)
                pool.wait_ge(sidx_copied, i + 1)
                pool.reg_add(bound, zero, S * TOPK - 1)
                nc.gpsimd.indirect_dma_start(out=y_d[:, :], out_offset=bass.IndirectOffsetOnAxis(ap=sidx[:, 0:1], axis=0),
                                             in_=yout, in_offset=None,
                                             bounds_check=bound, oob_is_err=False).then_inc(scattered, 16)
                pool.wait_ge(scattered, i * 16 + 16)
                pool.sem_inc(yout_free, 1)

            pool.wait_ge(tn_out, 16 * TT)
            pool.wait_ge(logits_done, TT)
            nc.gpsimd.memset(gath, 0.0).then_inc(gath_zero, 1)
            pool.sem_inc(yout_free, 1)
            pool.wait_ge(gath_zero, 1)
            pool.wait_ge(tables, 1)
            for i in range(3):
                gather(i)
            with pool.Fori(2, E - 1) as i:
                scatter(i - 2)
                gather(i + 1)
            for i in range(E - 3, E):
                scatter(i)
            n_over = pool.value_load(novi[0:1, 0:1], min_val=0, max_val=OVER)
            with pool.If(n_over > 0):
                gather(E)
                gather(E + 1)
                with pool.Fori(E + 1, ITEMS - 1) as i:
                    gather(i + 1)
                    scatter(i - 1)
                for i in range(ITEMS - 2, ITEMS):
                    scatter(i)
            nc.gpsimd.memset(gidx[:], 0).then_inc(all_scattered, 1)

        @block.scalar
        def _(act):
            def hi(dst, src, wait_full, wait_used):
                if wait_full is not None:
                    act.wait_ge(*wait_full)
                if wait_used is not None:
                    act.wait_ge(used, wait_used)
                nc.scalar.copy(dst, src).then_inc(split_hi, 1)

            def hi_early(g):
                z = g // 2 if g < W_IN_PIECES else 5 + (g - W_IN_PIECES) // 2
                hi(stage_hi[:, g % STAGES, :], piece_ap(g),
                   (full[z], 16 if g < W_IN_PIECES else 32) if g % 2 == 0 else None,
                   g - STAGES + 1 if STAGES <= g < W_IN_PIECES + STAGES else None)

            for t in range(TT):
                act.wait_ge(x_in, 16 * (TT + 1))
                nc.scalar.activation(sqjunk, xs[t], ACT.Square, accum_out=ss1[:, t:t + 1]).then_inc(h_sq, 1)
                act.wait_ge(h_sq, t + 1)
            act.wait_ge(consts, 2)
            nc.scalar.activation(rs1, ss1, ACT.Sqrt, scale=1.0 / D, bias=epsc).then_inc(h_sq, 1)
            act.wait_ge(vec_in, 64)
            nc.scalar.copy(wfr[:, 0, :], wfraw[:].rearrange("p k h -> p (k h)")).then_inc(f_split, 1)
            for j in range(2 * TT):
                t, h = j // 2, j % 2
                act.wait_ge(h_turned, j + 1)
                nc.scalar.copy(hT_hi[:, 4 * h:4 * h + 4, t * P:(t + 1) * P],
                               bank[4 + j % 4][:].rearrange("p (k t) -> p k t", k=4)).then_inc(h_hi, 1)
                if j == 3:
                    for g in range(STAGES):
                        hi_early(g)

            def qk_evac(group):
                tile0 = {0: 0, 1: 4, 3: 8, 4: 12}[group]
                act.wait_ge(used, 4 * group + 4)
                for c in range(4):
                    nc.scalar.activation(qk[:, tile0 + c, :], bank[4 * (group % 2) + c][:], ACT.Copy,
                                         scale=HD ** -0.5 if group in (0, 3) else 1.0).then_inc(qk_copied, 1)

            for group in range(6):
                for g in range(4 * (group + 1), 4 * (group + 2)):
                    if g < W_IN_PIECES:
                        hi_early(g)
                if group not in (2, 5):
                    qk_evac(group)
            nc.scalar.preload_act_table_set("natural_log_exp_and_others")
            act.wait_ge(f_steps, 2)
            nc.scalar.activation(negc, negc, ACT.Exp).then_inc(f_steps, 1)
            act.wait_ge(f_steps, 3)
            nc.scalar.activation(negc, negc, ACT.Ln, bias=1.0).then_inc(f_steps, 1)

            def sb_exp(u):
                n = (u % TT + 1) * P
                act.wait_ge(loga_ready, u + 1)
                if u >= 2:
                    act.wait_ge(pvs_done, u - 1)
                nc.scalar.activation(abuf[:, u % 2, 0:n], bank[3 + u % 3][:, 0:n], ACT.Exp).then_inc(a_ready, 1)

            def mix_evac(n):
                half = slice(64 * (n % 2), 64 * (n % 2) + 64)
                for kind, b, done in ((0, 6, pvf_done), (1, 7, pvs_done)):
                    act.wait_ge(done, TT * (n + 1))
                    c = 4 * kind + n // 2
                    nc.scalar.activation(hT_hi[half, c, :], bank[b][half, :], ACT.Copy,
                                         scale=gmix[half, c:c + 1]).then_inc(mix_hi, 1)
                    nc.scalar.activation(qk[half, 8 * kind + n // 2, :], bank[b][half, :], ACT.Square).then_inc(mix_sq, 1)

            for u in range(UNITS + 2):
                if u < UNITS:
                    n = (u % TT + 1) * P
                    act.wait_ge(neg_ready, u + 1)
                    if u >= 2:
                        act.wait_ge(pt_turned, u - 1)
                    nc.scalar.activation(pbuf[:, u % 2, 0:n], bank[u % 2][:, 0:n], ACT.Exp,
                                         bias=negmax[:, u % 2:u % 2 + 1],
                                         accum_out=rsum[:, u % 2:u % 2 + 1]).then_inc(p_ready, 1)
                    act.wait_ge(z_ready, u + 1)
                    if u >= 2:
                        act.wait_ge(sp_ready, u - 1)
                    nc.scalar.activation(lbuf[:, u % 2, 0:n], bank[3 + u % 3][:, 0:n], ACT.Abs).then_inc(absz, 1)
                    act.wait_ge(absz, u + 1)
                    nc.scalar.activation(lbuf[:, u % 2, 0:n], lbuf[:, u % 2, 0:n], ACT.Exp, scale=-1.0).then_inc(e_ready, 1)
                    act.wait_ge(e_ready, u + 1)
                    nc.scalar.activation(lbuf[:, u % 2, 0:n], lbuf[:, u % 2, 0:n], ACT.Ln, bias=1.0).then_inc(ln_ready, 1)
                if 1 <= u <= UNITS:
                    sb_exp(u - 1)
                if u >= 5 and (u - 5) % TT == 0:
                    mix_evac((u - 5) // TT)
            for g in range(W_IN_PIECES, W_IN_PIECES + 4):
                hi_early(g)
            act.wait_ge(ssm_done, 1)
            nc.scalar.activation(rsm, bank[0][:, 0:8], ACT.Sqrt, scale=1.0 / HW, bias=epsc).then_inc(rsm_ready, 1)
            act.wait_ge(oproj, 8)
            for g in range(W_IN_PIECES + 4, MOE0):
                hi_early(g)
            for t in range(TT):
                act.wait_ge(x2_add, 2 * TT + 2 * t + 2)
                nc.scalar.activation(tn[t], x2[t], ACT.Square, accum_out=ss2[:, t:t + 1]).then_inc(x2_sq, 1)
                act.wait_ge(x2_sq, t + 1)
                nc.scalar.activation(rs2[:, t:t + 1], ss2[:, t:t + 1], ACT.Sqrt, scale=1.0 / D, bias=epsc).then_inc(x2_rs, 1)
            for t in range(TT):
                for h in range(2):
                    act.wait_ge(tn_turned, 2 * t + h + 1)
                    if t >= 1:
                        act.wait_ge(logits_done, t)
                    nc.scalar.copy(tT[:, 4 * h:4 * h + 4, :], bank[6 + h][:].rearrange("p (k t) -> p k t", k=4)).then_inc(tT_copied, 1)
            act.wait_ge(bias_in, 64)
            act.wait_ge(oproj, 16)
            nc.scalar.copy(bias1, slot(7)[0:64, :]).then_inc(bias_hi, 1)
            nc.scalar.copy(bias2, slot(8)[0:64, 0:D]).then_inc(bias_hi, 1)
            act.wait_ge(exp4, 1)
            nc.scalar.activation(rt[:, 0:16], rt[:, 0:16], ACT.Exp).then_inc(exp4, 1)
            nc.scalar.preload_act_table_set("sigmoid_and_others")

            def hi_moe(j, z, turns, used_at):
                h = j % 2
                hi(stage_hi[:, j % STAGES, :], slot(z)[:, h * PIECE:(h + 1) * PIECE],
                   (full[z], turns) if h == 0 else None, used_at)

            def x_evac(t):
                act.wait_ge(x_turned, t + 1)
                for h in range(2):
                    nc.scalar.copy(xT_hi[:, 4 * h:4 * h + 4, :], bank[6 + h][:].rearrange("p (k t) -> p k t", k=4)).then_inc(xT_hi_r, 1)

            def a_evac(t):
                act.wait_ge(a_turned, t + 1)
                for h in range(2):
                    nc.scalar.copy(aT_hi[:, 4 * h:4 * h + 4, :], bank[6 + h][:].rearrange("p (k t) -> p k t", k=4)).then_inc(aT_hi_r, 1)

            def sigmoid(t):
                act.wait_ge(clipped, 2 * t + 1)
                wait(act, act_made, t)
                nc.scalar.activation(sig, glu, ACT.Sigmoid, scale=ALPHA).then_inc(sig_done, 1)

            def y_evac(t, used_at):
                act.wait_ge(used, used_at)
                act.wait_ge(yout_free, t + 1)
                act.wait_ge(weight_ready, t + 1)
                for h in range(2):
                    ins = nc.scalar.activation(yout[:, h * BANK:(h + 1) * BANK], bank[4 + h][:], ACT.Copy,
                                               scale=wcol[:])
                ins.then_inc(y_ready, 1)

            def run_items(run):
                q0, n, b, T0 = run.first, run.n, run.base, run.turn0
                ub = b - OPROJ_PIECES

                def turns(z, k):
                    return 16 * (loads_before(z) + k)

                x_evac(q0)
                for j in range(W1P):
                    z = moe_slot(j // 2)
                    if b == MOE0 and j < STAGES:
                        hi_moe(j, z, turns(z, T0 + 1), None)
                    else:
                        hi_moe(j, z, turns(z, T0 + 1), ub + j - STAGES + 1)
                sigmoid(q0)
                x_evac(q0 + 1)

                def body(r, first=False, last=False):
                    t = r + q0
                    for j in range(W1P + W2P):
                        s = j // 2
                        z = (s + 5) % SLOTS
                        k = T0 if s < 4 else T0 + 1
                        hi_moe(j, z, r * 16 + turns(z, k), r * 24 + (ub - 8 + j - STAGES + 1))
                        if j == 3 and not first:
                            y_evac(t - 2, r * 24 + (ub - 8))
                        if j == 9:
                            a_evac(t - 1)
                        if j == 19:
                            sigmoid(t)
                        if j == 20 and not last:
                            x_evac(t + 1)
                body(1, first=True)
                with act.Fori(2, n - 1) as r:
                    body(r)
                body(n - 1, last=True)
                y_evac(q0 + n - 2, ub + 24 * n - 8)
                a_evac(q0 + n - 1)
                for j in range(W2P):
                    c = (24 * n - 8) // 2 + j // 2
                    z = moe_slot(c)
                    hi_moe(j, z, turns(z, T0 + c // SLOTS + 1), ub + 24 * n - 8 + j - STAGES + 1)
                y_evac(q0 + n - 1, ub + 24 * n)

            run_items(MAIN)
            act.wait_ge(tables, 1)
            n_over = act.value_load(novi[0:1, 0:1], min_val=0, max_val=OVER)
            with act.If(n_over > 0):
                run_items(REST)
            for t in range(TT):
                act.wait_ge(fin_sum, t * 4 + 4)
                nc.scalar.activation(ring[:, t * 5 * D + D:t * 5 * D + 2 * D], ring[:, t * 5 * D:t * 5 * D + D],
                                     ACT.Square, accum_out=ss3[:, t:t + 1]).then_inc(fin_sq, 1)
                act.wait_ge(fin_sq, t + 1)
                nc.scalar.activation(rs3[:, t:t + 1], ss3[:, t:t + 1], ACT.Sqrt, scale=1.0 / D, bias=epsc).then_inc(fin_rs, 1)

        @block.vector
        def _(dve):
            def chained(ins):
                link(dve, "dve", ins)

            def lo(dst, src, hi_ap, g1):
                dve.wait_ge(split_hi, g1)
                nc.vector.tensor_tensor(dst, src, hi_ap.bitcast(F32), ALU.subtract).then_inc(split_lo, 1)

            def lo_early(g):
                lo(stage_lo[:, g % STAGES, :], piece_ap(g), stage_hi[:, g % STAGES, :], g + 1)

            dve.wait_ge(h_sq, TT + 1)
            chained(nc.vector.reciprocal(r1, rs1))
            for t in range(TT):
                nc.vector.scalar_tensor_tensor(out=xs[t], in0=xs[t], scalar=r1[:, t:t + 1], in1=g1b,
                                               op0=ALU.mult, op1=ALU.mult).then_inc(h_norm, 1)
            dve.wait_ge(f_split, 1)
            nc.vector.tensor_tensor(wfr[:, 1, :], wfraw[:].rearrange("p k h -> p (k h)"), wfr[:, 0, :].bitcast(F32),
                                    ALU.subtract).then_inc(f_split, 1)
            for j in range(2 * TT):
                t, h = j // 2, j % 2
                dve.wait_ge(h_hi, j + 1)
                a = (slice(None), slice(4 * h, 4 * h + 4), slice(t * P, (t + 1) * P))
                nc.vector.tensor_tensor(hT_lo[a], bank[4 + j % 4][:].rearrange("p (k t) -> p k t", k=4),
                                        hT_hi[a].bitcast(F32), ALU.subtract).then_inc(h_lo, 1)
                if j == 3:
                    for g in range(STAGES):
                        lo_early(g)

            def v_evac(group):
                dve.wait_ge(used, 4 * group + 4)
                for t in range(TT):
                    o = 0 if group == 2 else HW
                    nc.vector.tensor_copy(vbuf[:, t, o:o + HW], bank[4 * (group % 2) + t][:]).then_inc(v_copied, 1)

            for group in range(6):
                for g in range(4 * (group + 1), 4 * (group + 2)):
                    if g < W_IN_PIECES:
                        lo_early(g)
                if group in (2, 5):
                    v_evac(group)
            dve.wait_ge(f_mm, 1)
            dve.wait_ge(consts, 14)
            fu, m = csum, spbuf[0:NH, 0:S]
            nc.vector.tensor_scalar(fu, bank[0][0:NH, :], bfc, None, ALU.add).then_inc(f_steps, 1)
            dve.wait_ge(f_steps, 1)
            nc.vector.scalar_tensor_tensor(out=negc, in0=fu, scalar=-1.0, in1=fu, op0=ALU.mult, op1=ALU.min).then_inc(f_steps, 1)
            chained(nc.vector.tensor_scalar(m, fu, -1.0, 0.0, ALU.mult, ALU.max))
            dve.wait_ge(f_steps, 4)
            nc.vector.tensor_tensor_scan(fu, m, negc, 0.0, ALU.add, ALU.add).then_inc(negc_ready, 1)

            def sp_ap(u):
                i = u % TT
                o = 1280 * (u // TT % 2) + P * i * (i + 1) // 2
                return spbuf[:, o:o + P * (i + 1)]

            def mix_lo_part(n):
                half = slice(64 * (n % 2), 64 * (n % 2) + 64)
                for kind in range(2):
                    c = 4 * kind + n // 2
                    dve.wait_ge(mix_sq, 2 * n + kind + 1)
                    nc.vector.scalar_tensor_tensor(out=hT_lo[half, c, :], in0=bank[6 + kind][half, :],
                                                   scalar=gmix[half, c:c + 1], in1=hT_hi[half, c, :].bitcast(F32),
                                                   op0=ALU.mult, op1=ALU.subtract).then_inc(mix_lo, 1)

            for u in range(UNITS + 2):
                if u < UNITS:
                    n = (u % TT + 1) * P
                    dve.wait_ge(s_ready, u + 1)
                    if u >= 2:
                        dve.wait_ge(neg_ready, u - 1)
                    chained(nc.vector.tensor_reduce(smax[:, u % 2:u % 2 + 1], bank[u % 2][:, 0:n], AX.X, ALU.max))
                    if u >= 2:
                        dve.wait_ge(p_ready, u - 1)
                    nc.vector.tensor_scalar(negmax[:, u % 2:u % 2 + 1], smax[:, u % 2:u % 2 + 1], -1.0, None, ALU.mult).then_inc(neg_ready, 1)
                if 1 <= u <= UNITS:
                    v = u - 1
                    n = (v % TT + 1) * P
                    dve.wait_ge(p_ready, v + 1)
                    chained(nc.vector.reciprocal(rinv[:, v % 2:v % 2 + 1], rsum[:, v % 2:v % 2 + 1]))
                    nc.vector.tensor_scalar(pbuf[:, v % 2, 0:n], pbuf[:, v % 2, 0:n], rinv[:, v % 2:v % 2 + 1], None,
                                            ALU.mult).then_inc(ps_ready, 1)
                    dve.wait_ge(ln_ready, v + 1)
                    if v >= 8:
                        dve.wait_ge(loga_ready, TT * (v // TT - 1))
                    nc.vector.scalar_tensor_tensor(out=sp_ap(v), in0=bank[3 + v % 3][:, 0:n], scalar=0.0,
                                                   in1=lbuf[:, v % 2, 0:n], op0=ALU.max, op1=ALU.add).then_inc(sp_ready, 1)
                    dve.wait_ge(pt_turned, v + 1)
                    if v >= 2:
                        dve.wait_ge(pvf_done, v - 1)
                    nc.vector.tensor_copy(ptbuf[:, v % 2, 0:n], bank[2][:, 0:n]).then_inc(pt_ready, 1)
                if u >= 5 and (u - 5) % TT == 0:
                    mix_lo_part((u - 5) // TT)
            for g in range(W_IN_PIECES, W_IN_PIECES + 4):
                lo_early(g)
            dve.wait_ge(rsm_ready, 1)
            chained(nc.vector.reciprocal(rm, rsm))
            dve.wait_ge(x2_in, 16 * TT)
            for half in range(2):
                for j in range(8):
                    t, h = j // 2, j % 2
                    dve.wait_ge(oproj, 8 * half + j + 1)
                    if half:
                        dve.wait_ge(x2_add, j + 1)
                    dst = x2[t][:, h * BANK:(h + 1) * BANK]
                    nc.vector.scalar_tensor_tensor(out=dst, in0=bank[j][:], scalar=rm[:, 4 * half + t:4 * half + t + 1],
                                                   in1=dst, op0=ALU.mult, op1=ALU.add).then_inc(x2_add, 1)
                if half == 0:
                    for g in range(W_IN_PIECES + 4, MOE0):
                        lo_early(g)
            dve.wait_ge(g2_in, 16)
            for t in range(TT):
                dve.wait_ge(x2_rs, t + 1)
                chained(nc.vector.reciprocal(r2[:, t:t + 1], rs2[:, t:t + 1]))
                nc.vector.scalar_tensor_tensor(out=tn[t], in0=x2[t], scalar=r2[:, t:t + 1], in1=g2b,
                                               op0=ALU.mult, op1=ALU.mult).then_inc(tn_ready, 1)

            def part(o, n):
                return rt[:, o:o + n]
            w4 = part(0, 16)
            v8 = part(16, 32)
            i8 = part(48, 32).bitcast(U32)
            kf = part(80, 16)
            lg = part(96, 128)
            oh = part(224, 512).rearrange("p (a e) -> p a e", e=E)
            M = part(736, 128)
            pos = part(864, 128)
            cnt = part(992, 32)
            nov = part(1024, 32)
            incl = part(1056, 32)
            oba = part(1088, 32)
            jj = part(1120, 128)
            g1 = part(1248, 128)
            Bv = part(1376, 32)
            item = part(1408, 128)
            slt = part(1536, 128)
            sumw = part(1664, 4)
            item_k = part(1668, 16)
            slot_k = part(1684, 16)
            eidx = part(1700, ITEMS)
            tmp = part(1747, 47)
            tmp2 = part(1794, 47)
            dve.wait_ge(logits_done, TT)
            for t in range(TT):
                chained(nc.vector.tensor_copy(lg[:, t * E:(t + 1) * E], bank[4][:, t * E:(t + 1) * E]))
                chained(nc.vector.max(v8[:, 8 * t:8 * t + 8], lg[:, t * E:(t + 1) * E]))
                chained(nc.vector.max_index(i8[:, 8 * t:8 * t + 8], v8[:, 8 * t:8 * t + 8], lg[:, t * E:(t + 1) * E]))
            v84 = v8.rearrange("p (t k) -> p t k", k=8)
            w44 = w4.rearrange("p (t k) -> p t k", k=TOPK)
            nc.vector.tensor_tensor(w44, v84[:, :, 0:4], v84[:, :, 0:1].to_broadcast([P, TT, TOPK]), ALU.subtract).then_inc(exp4, 1)
            chained(nc.vector.tensor_copy(kf.rearrange("p (t k) -> p t k", k=TOPK),
                                          i8.rearrange("p (t k) -> p t k", k=8)[:, :, 0:4]))
            iota_e = iotas[:, 0:E]
            chained(nc.vector.tensor_tensor(oh, iota_e.unsqueeze(1).to_broadcast([P, 16, E]),
                                            kf.unsqueeze(2).to_broadcast([P, 16, E]), ALU.is_equal))
            nc.vector.tensor_reduce(M.rearrange("p (t e) -> p t e", e=E),
                                    oh.rearrange("p (t k) e -> p t e k", k=TOPK), AX.X, ALU.add).then_inc(onehots, 1)
            dve.wait_ge(bias_hi, 2)
            nc.vector.tensor_tensor(bias1[32:64, :], slot(7)[32:64, :], bias1[32:64, :].bitcast(F32), ALU.subtract).then_inc(bias_lo, 1)
            nc.vector.tensor_tensor(bias2[32:64, :], slot(8)[32:64, 0:D], bias2[32:64, :].bitcast(F32), ALU.subtract).then_inc(bias_lo, 1)
            dve.wait_ge(counted, 1)
            chained(nc.vector.tensor_copy(pos, bank[5][:, 0:128]))
            chained(nc.vector.tensor_copy(cnt, bank[5][:, 128:160]))
            chained(nc.vector.tensor_scalar(nov, cnt, float(P), None, ALU.is_gt))
            for j in (2, 3):
                chained(nc.vector.scalar_tensor_tensor(out=nov, in0=cnt, scalar=float(j * P), in1=nov, op0=ALU.is_gt, op1=ALU.add))
            chained(nc.vector.tensor_tensor_scan(incl, nov, ones[:, 0:E], 0.0, ALU.add, ALU.mult))
            chained(nc.vector.tensor_tensor(oba, incl, nov, ALU.subtract))
            chained(nc.vector.tensor_scalar(g1, pos, float(P), None, ALU.is_ge))
            chained(nc.vector.scalar_tensor_tensor(out=jj, in0=pos, scalar=2.0 * P, in1=g1, op0=ALU.is_ge, op1=ALU.add))
            chained(nc.vector.scalar_tensor_tensor(out=jj, in0=pos, scalar=3.0 * P, in1=jj, op0=ALU.is_ge, op1=ALU.add))
            chained(nc.vector.scalar_tensor_tensor(out=slt, in0=jj, scalar=-float(P), in1=pos, op0=ALU.mult, op1=ALU.add))
            chained(nc.vector.scalar_tensor_tensor(out=Bv, in0=oba, scalar=E - 1.0, in1=iota_e, op0=ALU.add, op1=ALU.subtract))
            i3 = item.rearrange("p (t e) -> p t e", e=E)
            chained(nc.vector.tensor_tensor(i3, g1.rearrange("p (t e) -> p t e", e=E), Bv.unsqueeze(1).to_broadcast([P, TT, E]), ALU.mult))
            chained(nc.vector.tensor_tensor(i3, i3, iota_e.unsqueeze(1).to_broadcast([P, TT, E]), ALU.add))
            chained(nc.vector.tensor_tensor(item, item, jj, ALU.add))
            pick = spbuf[:, 2048:2560].rearrange("p (t k e) -> p t k e", t=TT, k=TOPK)
            oh4 = oh.rearrange("p (t k) e -> p t k e", k=TOPK)
            for src, dst in ((item, item_k), (slt, slot_k)):
                for t in range(TT):
                    chained(nc.vector.tensor_tensor(pick[:, t], oh4[:, t], src[:, t * E:(t + 1) * E].unsqueeze(1).to_broadcast([P, TOPK, E]), ALU.mult))
                chained(nc.vector.tensor_reduce(dst.rearrange("p (t k) -> p t k", k=TOPK), pick, AX.X, ALU.add))
            dve.wait_ge(exp4, 2)
            chained(nc.vector.tensor_reduce(sumw, w44, AX.X, ALU.add))
            chained(nc.vector.reciprocal(sumw, sumw))
            chained(nc.vector.tensor_tensor(w44, w44, sumw.unsqueeze(2).to_broadcast([P, TT, TOPK]), ALU.mult))
            chained(nc.vector.tensor_tensor(ohslot, iotas[:].unsqueeze(1).to_broadcast([P, 16, P]),
                                            slot_k.unsqueeze(2).to_broadcast([P, 16, P]), ALU.is_equal))
            dve.wait_ge(tn_out, 16 * TT)
            chained(nc.vector.tensor_tensor(payload[:, :, 1, :], iotas[:, 0:ITEMS].unsqueeze(1).to_broadcast([P, 16, ITEMS]),
                                            item_k.unsqueeze(2).to_broadcast([P, 16, ITEMS]), ALU.is_equal))
            chained(nc.vector.tensor_tensor(payload[:, :, 0, :], payload[:, :, 1, :],
                                            row1.unsqueeze(2).to_broadcast([P, 16, ITEMS]), ALU.mult))
            nc.vector.tensor_tensor(payload[:, :, 1, :], payload[:, :, 1, :],
                                    w4.unsqueeze(2).to_broadcast([P, 16, ITEMS]), ALU.mult).then_inc(slots_ready, 1)
            chained(nc.vector.tensor_copy(eidx[:, 0:E], iota_e))
            ra = oh.rearrange("p a e -> p (a e)")[:, 0:OVER * E].rearrange("p (i e) -> p i e", e=E)
            rb = pick.rearrange("p t k e -> p (t k e)")[:, 0:OVER * E].rearrange("p (i e) -> p i e", e=E)
            io = iotas[:, 0:OVER].unsqueeze(2).to_broadcast([P, OVER, E])
            chained(nc.vector.tensor_tensor(ra, io, oba.unsqueeze(1).to_broadcast([P, OVER, E]), ALU.is_ge))
            chained(nc.vector.tensor_tensor(rb, io, incl.unsqueeze(1).to_broadcast([P, OVER, E]), ALU.is_lt))
            chained(nc.vector.tensor_tensor(ra, ra, rb, ALU.mult))
            chained(nc.vector.tensor_tensor(ra, ra, iota_e.unsqueeze(1).to_broadcast([P, OVER, E]), ALU.mult))
            chained(nc.vector.tensor_reduce(eidx[:, E:ITEMS], ra, AX.X, ALU.add))
            chained(nc.vector.tensor_copy(eidtab[0:1, 0:OVER], eidx[0:1, E:ITEMS]))
            chained(nc.vector.tensor_copy(novi[:], incl[0:1, E - 1:E]))
            chained(nc.vector.tensor_scalar(seltab[:], eidx[0:64, :], pmod, None, ALU.is_equal))
            dve.wait_ge(tab_mm, 1)
            chained(nc.vector.tensor_copy(wtab[:], bank[5][:, 256 + ITEMS:256 + 2 * ITEMS]))
            chained(nc.vector.tensor_scalar(tmp, bank[5][:, 256:256 + ITEMS], 0.0, EMPTY, ALU.is_equal, ALU.mult))
            chained(nc.vector.scalar_tensor_tensor(out=tmp2, in0=bank[5][:, 256:256 + ITEMS], scalar=-1.0, in1=tmp,
                                                   op0=ALU.add, op1=ALU.add))
            chained(nc.vector.tensor_copy(stab[:], tmp2))
            nc.vector.tensor_scalar(gtab[:], stab[:], 2, None, ALU.arith_shift_right).then_inc(tables, 1)

            def lo_moe(j, z, at):
                h = j % 2
                lo(stage_lo[:, j % STAGES, :], slot(z)[:, h * PIECE:(h + 1) * PIECE], stage_hi[:, j % STAGES, :], at)

            def turned_lo(dst_lo, dst_hi, ready, done, t):
                for h in range(2):
                    dve.wait_ge(ready, t * 2 + (h + 1))
                    nc.vector.tensor_tensor(dst_lo[:, 4 * h:4 * h + 4, :], bank[6 + h][:].rearrange("p (k t) -> p k t", k=4),
                                            dst_hi[:, 4 * h:4 * h + 4, :].bitcast(F32), ALU.subtract).then_inc(done, 1)

            def at_col(tab, i, rows=P):
                return tab[0:rows, i:i + 1] if isinstance(i, int) else tab[0:rows, bass.ds(i, 1)]

            def select1(i):
                wait(dve, sel1_used, i)
                nc.vector.tensor_copy(sel1, at_col(seltab, i, 64).to_broadcast([64, P])).then_inc(sel1_r, 1)

            def select2(i, used_at):
                dve.wait_ge(used, used_at)
                nc.vector.tensor_copy(sel2, at_col(seltab, i, 64).to_broadcast([64, P])).then_inc(sel2_r, 1)

            def weights(i):
                wait(dve, y_ready, i)
                nc.vector.tensor_copy(wcol[:], at_col(wtab, i)).then_inc(weight_ready, 1)

            def clip(t, part_, used_at):
                if part_ == 0:
                    dve.wait_ge(used, used_at)
                    wait(dve, act_made, t)
                    for h in range(2):
                        ins = nc.vector.tensor_scalar(glu[:, h * BANK:(h + 1) * BANK], bank[h][:], LIMIT, None, ALU.min)
                else:
                    wait(dve, a_turned, t)
                    for h in range(2):
                        ins = nc.vector.tensor_scalar(lin[:, h * BANK:(h + 1) * BANK], bank[2 + h][:], LIMIT, -LIMIT,
                                                      ALU.min, ALU.max)
                ins.then_inc(clipped, 1)

            def gated(t):
                dve.wait_ge(sig_done, t + 1)
                nc.vector.tensor_tensor(sig, sig, glu, ALU.mult).then_inc(gs_made, 1)
                dve.wait_ge(gs_made, t + 1)
                dve.wait_ge(clipped, t * 2 + 2)
                nc.vector.scalar_tensor_tensor(out=lin, in0=lin, scalar=1.0, in1=sig, op0=ALU.add, op1=ALU.mult).then_inc(act_made, 1)

            def run_items(run):
                q0, n, b = run.first, run.n, run.base
                ub = b - OPROJ_PIECES
                select1(q0)
                turned_lo(xT_lo, xT_hi, xT_hi_r, xT_lo_r, q0)
                for j in range(W1P):
                    lo_moe(j, moe_slot(j // 2), b + j + 1)
                    if j == 2:
                        select2(q0, ub)
                        weights(q0)
                    if j == 4:
                        select1(q0 + 1)
                clip(q0, 0, ub + W1P)
                clip(q0, 1, ub + W1P)
                turned_lo(xT_lo, xT_hi, xT_hi_r, xT_lo_r, q0 + 1)

                def body(r, first=False, last=False):
                    t = r + q0
                    for j in range(W1P + W2P):
                        lo_moe(j, (j // 2 + 5) % SLOTS, r * 24 + (b - 8 + j + 1))
                        if j == 1:
                            gated(t - 1)
                        if j == 5 and not first:
                            select2(t - 1, r * 24 + (ub - 8))
                            weights(t - 1)
                        if j == 7 and not last:
                            select1(t + 1)
                        if j == 9:
                            turned_lo(aT_lo, aT_hi, aT_hi_r, aT_lo_r, t - 1)
                        if j == 17:
                            clip(t, 0, r * 24 + (ub - 8 + W1P))
                        if j == 18:
                            clip(t, 1, None)
                        if j == 20 and not last:
                            turned_lo(xT_lo, xT_hi, xT_hi_r, xT_lo_r, t + 1)
                body(1, first=True)
                with dve.Fori(2, n - 1) as r:
                    body(r)
                body(n - 1, last=True)
                gated(q0 + n - 1)
                turned_lo(aT_lo, aT_hi, aT_hi_r, aT_lo_r, q0 + n - 1)
                for j in range(W2P):
                    c = (24 * n - 8) // 2 + j // 2
                    lo_moe(j, moe_slot(c), b + 24 * n - 8 + j + 1)
                    if j == 0:
                        select2(q0 + n - 1, ub + 24 * n - 8)
                        weights(q0 + n - 1)

            dve.wait_ge(x2_out, 16 * TT)
            run_items(MAIN)
            n_over = dve.value_load(novi[0:1, 0:1], min_val=0, max_val=OVER)
            with dve.If(n_over > 0):
                run_items(REST)

            dve.wait_ge(gf_in, 16)
            for t in range(TT):
                o = t * 5 * D
                dve.wait_ge(fin_in, 32 * TT)
                acc = ring[:, o:o + D]
                for j in range(TOPK):
                    nc.vector.tensor_tensor(acc, acc, ring[:, o + (j + 1) * D:o + (j + 2) * D], ALU.add).then_inc(fin_sum, 1)
                    dve.wait_ge(fin_sum, 4 * t + j + 1)
            for t in range(TT):
                acc = ring[:, t * 5 * D:t * 5 * D + D]
                dve.wait_ge(fin_rs, t + 1)
                chained(nc.vector.reciprocal(r3[:, t:t + 1], rs3[:, t:t + 1]))
                nc.vector.scalar_tensor_tensor(out=acc, in0=acc, scalar=r3[:, t:t + 1], in1=gfb, op0=ALU.mult,
                                               op1=ALU.mult).then_inc(fin_ready, 1)

        @block.tensor
        def _(pe):
            def three(dst, w_hi, w_lo, m_hi, m_lo, start, stop):
                pe.matmul(dst, w_hi, m_hi, start=start, stop=False)
                pe.matmul(dst, w_hi, m_lo, start=False, stop=False)
                return pe.matmul(dst, w_lo, m_hi, start=False, stop=stop)

            pe.wait_ge(consts, 1)
            for j in range(2 * TT):
                t, h = j // 2, j % 2
                pe.wait_ge(h_norm, t + 1)
                if j >= 4:
                    pe.wait_ge(h_lo, j - 3)
                for k in range(4):
                    mm = pe.transpose(bank[4 + j % 4][:, k * P:(k + 1) * P], xs[t][:, (4 * h + k) * P:(4 * h + k + 1) * P], identF[:])
                mm.then_inc(h_turned, 1)
            pe.wait_ge(h_lo, 2 * TT)

            for group in range(6):
                banks = bank[4 * (group % 2):4 * (group % 2) + 4]
                if group >= 2:
                    if group == 4:
                        pe.wait_ge(v_copied, TT)
                    else:
                        pe.wait_ge(qk_copied, {2: 4, 3: 8, 5: 12}[group])
                for i in range(4):
                    g = 4 * group + i
                    pe.wait_ge(split_lo, g + 1)
                    whi = stage_hi[:, g % STAGES, :].rearrange("p (k n) -> p k n", k=2)
                    wlo = stage_lo[:, g % STAGES, :].rearrange("p (k n) -> p k n", k=2)
                    for kk in range(2):
                        k = 2 * i + kk
                        for c in range(4):
                            cs = slice(c * P, (c + 1) * P)
                            if group in (2, 5):
                                mm = three(banks[c][:], hT_hi[:, k, cs], hT_lo[:, k, cs], whi[:, kk, :], wlo[:, kk, :],
                                           k == 0, k == KT - 1)
                            else:
                                mm = three(banks[c][:], whi[:, kk, cs], wlo[:, kk, cs], hT_hi[:, k, :], hT_lo[:, k, :],
                                           k == 0, k == KT - 1)
                    mm.then_inc(used, 1)
                    if group == 5 and i == 1:
                        pe.wait_ge(qk_copied, 16)
                        pe.wait_ge(f_split, 2)
                        for k in range(KT):
                            fs = slice(k * NH, (k + 1) * NH)
                            mm = three(bank[0][0:NH, :], wfr[:, 0, fs], wfr[:, 1, fs], hT_hi[:, k, :], hT_lo[:, k, :],
                                       k == 0, k == KT - 1)
                        mm.then_inc(f_mm, 1)

            def scores(u):
                n, i = u // TT, u % TT
                half = slice(64 * (n % 2), 64 * (n % 2) + 64)
                dst = bank[u % 2][:, 0:(i + 1) * P]
                if u >= 2:
                    pe.wait_ge(p_ready, u - 1)
                pe.matmul(bank[u % 2][:, i * P:(i + 1) * P], identB[:], maskF[:], start=True, stop=False, skip_group_check=True)
                pe.matmul(dst, qk[half, n // 2, i * P:(i + 1) * P], qk[half, 4 + n // 2, 0:(i + 1) * P], start=False,
                          stop=False, skip_group_check=True)
                pe.matmul(dst, sel8[:, n, :], csum[:, 0:(i + 1) * P], start=False, stop=True,
                          skip_group_check=True).then_inc(s_ready, 1)

            def z_scores(u):
                n, j = u // TT, TT - 1 - u % TT
                half = slice(64 * (n % 2), 64 * (n % 2) + 64)
                b = bank[3 + u % 3]
                if u >= 3:
                    pe.wait_ge(a_ready, u - 2)
                pe.matmul(b[:, 0:P], identB[:], maskS[:], start=True, stop=False, skip_group_check=True)
                pe.matmul(b[:, 0:S - j * P], qk[half, 12 + n // 2, j * P:(j + 1) * P], qk[half, 8 + n // 2, j * P:S],
                          start=False, stop=True, skip_group_check=True).then_inc(z_ready, 1)

            def turn_p(u):
                i = u % TT
                pe.wait_ge(ps_ready, u + 1)
                if u >= 1:
                    pe.wait_ge(pt_ready, u)
                for kb in range(i + 1):
                    mm = pe.transpose(bank[2][:, kb * P:(kb + 1) * P], pbuf[:, u % 2, kb * P:(kb + 1) * P], identF[:])
                mm.then_inc(pt_turned, 1)

            def log_a(u):
                i = u % TT
                b = bank[3 + u % 3]
                pe.wait_ge(sp_ready, u + 1)
                for v in range(u - i, u + 1):
                    o = 1280 * (u // TT % 2) + P * (v % TT) * (v % TT + 1) // 2
                    w = P * (v % TT + 1)
                    mm = pe.matmul(b[:, (i + 1) * P - w:(i + 1) * P], (neg_tri if v == u else neg_one)[:], spbuf[:, o:o + w],
                                   start=False, stop=v == u, skip_group_check=True)
                mm.then_inc(loga_ready, 1)

            def pv_fox(u):
                n, i = u // TT, u % TT
                half = slice(64 * (n % 2), 64 * (n % 2) + 64)
                pe.wait_ge(pt_ready, u + 1)
                if i == 0 and n >= 2:
                    pe.wait_ge(mix_lo, 2 * (n - 1))
                    pe.wait_ge(mix_sq, 2 * (n - 1))
                for kb in range(i + 1):
                    mm = pe.matmul(bank[6][half, i * P:(i + 1) * P], vbuf[:, kb, n * HD:(n + 1) * HD],
                                   ptbuf[:, u % 2, kb * P:(kb + 1) * P], start=kb == 0, stop=kb == i)
                mm.then_inc(pvf_done, 1)

            def pv_stick(u):
                n, i = u // TT, u % TT
                j = TT - 1 - i
                half = slice(64 * (n % 2), 64 * (n % 2) + 64)
                pe.wait_ge(a_ready, u + 1)
                pe.matmul(bank[7][half, j * P:S], vbuf[:, j, HW + n * HD:HW + (n + 1) * HD], abuf[:, u % 2, 0:(i + 1) * P],
                          start=i == 0, stop=i == TT - 1, skip_group_check=True).then_inc(pvs_done, 1)

            pe.wait_ge(v_copied, 2 * TT)
            pe.wait_ge(qk_copied, 16)
            pe.wait_ge(negc_ready, 1)
            pe.wait_ge(consts, 14)
            for u in range(UNITS + 2):
                if u < UNITS:
                    scores(u)
                    z_scores(u)
                if 1 <= u <= UNITS:
                    turn_p(u - 1)
                    log_a(u - 1)
                if u >= 2:
                    pv_fox(u - 2)
                    pv_stick(u - 2)

            pe.wait_ge(mix_sq, 2 * NH)
            pe.wait_ge(mix_lo, 2 * NH)
            for kind in range(2):
                for t in range(TT):
                    for c in range(4):
                        mm = pe.matmul(bank[0][:, 4 * kind + t:4 * kind + t + 1], qk[:, 8 * kind + c, t * P:(t + 1) * P],
                                       ones[:, 0:1], start=c == 0, stop=c == 3)
            mm.then_inc(ssm_done, 1)
            for half in range(2):
                for i in range(4):
                    pe.wait_ge(split_lo, W_IN_PIECES + 4 * half + i + 1)
                for j in range(8):
                    t, h = j // 2, j % 2
                    if half:
                        pe.wait_ge(x2_add, j + 1)
                    if half == 0 and j == 0:
                        pe.wait_ge(rsm_ready, 1)
                    for i in range(4):
                        c = 4 * half + i
                        ts = slice(t * P, (t + 1) * P)
                        hs = slice(h * BANK, (h + 1) * BANK)
                        mm = three(bank[j][:], hT_hi[:, c, ts], hT_lo[:, c, ts], stage_hi[:, c % 4, hs], stage_lo[:, c % 4, hs],
                                   i == 0, i == 3)
                    mm.then_inc(oproj, 1)

            pe.wait_ge(x2_add, 16)
            pe.wait_ge(wrt_in, 32)
            for t in range(TT):
                pe.wait_ge(tn_ready, t + 1)
                for h in range(2):
                    if t >= 1:
                        pe.wait_ge(tT_copied, 2 * t - 1 + h)
                    for k in range(4):
                        mm = pe.transpose(bank[6 + h][:, k * P:(k + 1) * P], tn[t][:, (4 * h + k) * P:(4 * h + k + 1) * P], identF[:])
                    mm.then_inc(tn_turned, 1)
                pe.wait_ge(tT_copied, 2 * t + 2)
                for k in range(KT):
                    pe.matmul(bank[4][:, t * E:(t + 1) * E], tT[:, k, :], wrt[:, k, :], start=k == 0, stop=False)
                pe.matmul(bank[4][:, t * E:(t + 1) * E], ones[0:1, :], brt, start=False, stop=True).then_inc(logits_done, 1)
            pe.wait_ge(onehots, 1)
            M = rt[:, 736:864]
            for t in range(TT):
                for v in range(t + 1):
                    pe.matmul(bank[5][:, t * E:(t + 1) * E], (before if v == t else ones)[:], M[:, v * E:(v + 1) * E],
                              start=v == 0, stop=v == t)
            for v in range(TT):
                mm = pe.matmul(bank[5][:, 128:160], ones[:], M[:, v * E:(v + 1) * E], start=v == 0, stop=v == TT - 1)
            mm.then_inc(counted, 1)
            pe.wait_ge(slots_ready, 1)
            for a in range(16):
                mm = pe.matmul(bank[5][:, 256:256 + 2 * ITEMS], ohslot[:, a, :], payload[:, a].rearrange("p c n -> p (c n)"),
                               start=a == 0, stop=a == 15)
            mm.then_inc(tab_mm, 1)

            def turn_x(t):
                pe.wait_ge(gathered, t * 16 + 16)
                for k in range(KT):
                    mm = pe.transpose(bank[6 + k // 4][:, k % 4 * P:(k % 4 + 1) * P], gath[:, k * P:(k + 1) * P], identF[:])
                mm.then_inc(x_turned, 1)

            def turn_a(t):
                pe.wait_ge(act_made, t + 1)
                for k in range(KT):
                    mm = pe.transpose(bank[6 + k // 4][:, k % 4 * P:(k % 4 + 1) * P], lin[:, k * P:(k + 1) * P], identF[:])
                mm.then_inc(a_turned, 1)

            def bias_1(t):
                pe.wait_ge(sel1_r, t + 1)
                wait(pe, clipped, t * 2)
                for c in range(4):
                    mm = pe.matmul(bank[c][:], sel1, bias1[:, c * BANK:(c + 1) * BANK], start=True, stop=False)
                mm.then_inc(sel1_used, 1)

            def bias_2(t):
                pe.wait_ge(sel2_r, t + 1)
                wait(pe, y_ready, t)
                for c in range(2):
                    pe.matmul(bank[4 + c][:], sel2, bias2[:, c * BANK:(c + 1) * BANK], start=True, stop=False)

            def multiply(j, at, T_hi, T_lo, k, b0, stop):
                pe.wait_ge(split_lo, at)
                for (w, m) in ((T_hi, stage_hi), (T_hi, stage_lo), (T_lo, stage_hi)):
                    for h in range(2):
                        mm = pe.matmul(bank[b0 + h][:], w[:, k, :], m[:, j % STAGES, h * BANK:(h + 1) * BANK],
                                       start=False, stop=stop and w is T_lo)
                mm.then_inc(used, 1)

            def run_items(run):
                q0, n, b = run.first, run.n, run.base
                turn_x(q0)
                bias_1(q0)
                pe.wait_ge(xT_lo_r, 2 * q0 + 2)
                for j in range(W1P):
                    multiply(j, b + j + 1, xT_hi, xT_lo, j // 2, 2 * (j % 2), j // 2 == KT - 1)
                turn_x(q0 + 1)

                def body(r, last=False):
                    t = r + q0
                    bias_1(t)
                    pe.wait_ge(xT_lo_r, t * 2 + 2)
                    for j in range(W1P):
                        multiply(j, r * 24 + (b - 8 + j + 1), xT_hi, xT_lo, j // 2, 2 * (j % 2), j // 2 == KT - 1)
                        if j == 8:
                            turn_a(t - 1)
                    pe.wait_ge(aT_lo_r, t * 2)
                    if not last:
                        turn_x(t + 1)
                    bias_2(t - 1)
                    for j in range(W2P):
                        multiply(j, r * 24 + (b - 8 + W1P + j + 1), aT_hi, aT_lo, j, 4, j == KT - 1)
                body(1)
                with pe.Fori(2, n - 1) as r:
                    body(r)
                body(n - 1, last=True)
                turn_a(q0 + n - 1)
                pe.wait_ge(aT_lo_r, 2 * (q0 + n))
                bias_2(q0 + n - 1)
                for j in range(W2P):
                    multiply(j, b + 24 * n - 8 + j + 1, aT_hi, aT_lo, j, 4, j == KT - 1)

            pe.wait_ge(bias_lo, 2)
            run_items(MAIN)
            pe.wait_ge(tables, 1)
            n_over = pe.value_load(novi[0:1, 0:1], min_val=0, max_val=OVER)
            with pe.If(n_over > 0):
                run_items(REST)


_INS = ["x", "norm1_g", "w_in", "b_f", "g_fox", "g_sb", "w_out", "norm2_g", "w_router", "b_router",
        "w1", "b1", "w2", "b2", "norm_f_g"]


def kernel(**inputs):
    import numpy as np
    import concourse.bacc as bacc
    from concourse.bass_utils import run_bass_kernel_spmd

    nc = bacc.Bacc("TRN2", target_bir_lowering=False, num_devices=1)
    arrays, args = {}, []
    for name in _INS:
        a = np.ascontiguousarray(inputs[name])
        arrays[f"in_{name}"] = a
        args.append(nc.dram_tensor(f"in_{name}", a.shape, mybir.dt.from_np(a.dtype), kind="ExternalInput").ap())
    out = nc.dram_tensor("out", (1, S, D), F32, kind="ExternalOutput").ap()
    build(nc, *args, out)
    r = run_bass_kernel_spmd(nc, [arrays], core_ids=[0])
    return r.results[0]["out"]
```

```python
import concourse.bass as bass
from concourse import mybir
from contextlib import ExitStack

F32 = mybir.dt.float32
F32R = mybir.dt.float32r
BF16 = mybir.dt.bfloat16
I32 = mybir.dt.int32
U32 = mybir.dt.uint32
ACT = mybir.ActivationFunctionType
ALU = mybir.AluOpType
AX = mybir.AxisListType

P = 128
D = 1024
KT = D // P
S = 512
TT = S // P
NH = 8
HD = 64
HW = NH * HD
E = 32
TOPK = 4
EPS = 1e-5
LIMIT = 7.0
ALPHA = 1.702
MASKED = -1e30
BANK = 512
SLOT = 2048
SLOTS = 12
PIECE = 1024
STAGES = 4
UNITS = NH * TT
OVER = S * TOPK // P - 1
ITEMS = E + OVER
W_IN_PIECES = 2 * SLOTS
W_OUT_PIECES = KT
MOE0 = W_IN_PIECES + W_OUT_PIECES
OPROJ_PIECES = W_OUT_PIECES
W1P, W2P = 2 * KT, KT
EMPTY = 8192.0


WHOLE = 14
SPLIT = W1P + W2P - 2


def before_piece(j):
    return min(j, WHOLE) + max(j - WHOLE - 2, 0)


FILL0 = 2


def fill_at(q):
    return FILL0 + q // 3


def split_at(g):
    return FILL0 + -(-(g - 15) * 8 // 3)


def build(nc, x, norm1_g, w_in, b_f, g_fox, g_sb, w_out, norm2_g, w_router, b_router, w1, b1, w2, b2,
          norm_f_g, out):
    x_d, out_d = x[0], out[0]
    w_in_d, w_out_d, w_router_d = w_in[0], w_out[0], w_router[0]
    w1_d = w1[0].rearrange("e (k p) n -> e k p n", p=P)
    w2_d = w2[0].rearrange("e (k p) n -> e k p n", p=P)

    with ExitStack() as ctx:
        def sb(name, shape, dt=F32):
            return ctx.enter_context(nc.sbuf_tensor(name, shape, dt))

        def sem(name):
            return ctx.enter_context(nc.semaphore(name))

        tn_d = nc.dram_tensor("tn_scratch", (S, D), F32, kind="Internal").ap()
        x2_d = nc.dram_tensor("x2_scratch", (S, D), F32, kind="Internal").ap()
        y_d = nc.dram_tensor("y_scratch", (S * TOPK, D), F32, kind="Internal").ap()

        ring = sb("ring", [P, SLOTS * SLOT])
        stage_hi = sb("stage_hi", [P, STAGES, PIECE], F32R)
        stage_lo = sb("stage_lo", [P, STAGES, PIECE], F32R)
        act_hi = sb("act_hi", [P, KT * S], F32R)
        act_lo = sb("act_lo", [P, KT * S], F32R)
        qk = sb("qk", [P, 16, S])
        spr_hi = sb("spr_hi", [P, 1280], F32R)
        spr_lo = sb("spr_lo", [P, 1280], F32R)
        identF = sb("identF", [P, P])
        identB = sb("identB", [P, P], BF16)
        masks = sb("masks", [P, 2 * P], BF16)
        maskF = masks[:, 0:P]
        maskS = masks[:, P:2 * P]
        neg_tri = sb("neg_tri", [P, P], F32R)
        neg_one = sb("neg_one", [P, P], F32R)
        before = sb("before", [P, P], BF16)
        onesB = sb("onesB", [P, P], BF16)
        ones = sb("ones", [P, P])
        iotas = sb("iotas", [P, P])
        cols = sb("cols", [P, 104])
        gtab = sb("gtab", [P, ITEMS], I32)
        stab = sb("stab", [P, ITEMS], I32)
        wtab = sb("wtab", [P, ITEMS])
        seltab = sb("seltab", [64, ITEMS])
        eidtab = sb("eidtab", [1, 16], I32)
        novi = sb("novi", [1, 1], I32)
        gidx = sb("gidx", [P, 1], I32)
        sidx = sb("sidx", [P, 1], I32)
        wcol = sb("wcol", [P, 1])

        hT_hi = act_hi[:].rearrange("p (k t) -> p k t", k=KT)
        hT_lo = act_lo[:].rearrange("p (k t) -> p k t", k=KT)
        xT_hi = act_hi[:, 0:D].rearrange("p (k s) -> p k s", k=KT)
        xT_lo = act_lo[:, 0:D].rearrange("p (k s) -> p k s", k=KT)
        xT_7 = masks[:].bitcast(F32)
        aT_hi = act_hi[:, D:2 * D].rearrange("p (k s) -> p k s", k=KT)
        aT_lo = act_lo[:, D:2 * D].rearrange("p (k s) -> p k s", k=KT)
        bias1 = act_hi[0:64, 2 * D:4 * D]
        bias2 = act_lo[0:64, 2 * D:3 * D]
        sel1 = act_lo[0:64, 3 * D:3 * D + P]
        sel2 = act_lo[0:64, 3 * D + P:3 * D + 2 * P]

        def slot(z):
            return ring[:, z * SLOT:(z + 1) * SLOT]

        qk2 = qk[:].rearrange("p (a b) t -> p a (b t)", b=2)
        xs = [qk2[:, 4 + i, :] for i in range(TT)]
        g1b = qk2[:, 0, :]
        sqjunk = qk2[:, 1, :]
        vbuf = ring[:, 0:2 * SLOT].rearrange("p (t d) -> p t d", t=TT)
        ptbuf = slot(2)[:, 0:1024].rearrange("p (b n) -> p b n", b=2)
        spraw = slot(2)[:, 1024:2048].rearrange("p (b n) -> p b n", b=2)
        lbuf = slot(3)[:, 0:1024].rearrange("p (b n) -> p b n", b=2)
        abuf = slot(3)[:, 1024:2048].rearrange("p (b n) -> p b n", b=2)
        pbuf = slot(5).rearrange("p (b n) -> p b n", b=4)
        sel8 = slot(4)[0:NH, 0:NH * P].rearrange("p (h q) -> p h q", h=NH)
        negc = slot(4)[0:NH, 1024:1024 + S]
        csum = slot(4)[0:NH, 1536:1536 + S]
        fmax = slot(5)[0:NH, 1536:1536 + S]
        tri_raw, one_raw = slot(2)[:, 0:P], slot(2)[:, P:2 * P]
        sel8r = spr_hi[0:NH, 0:NH * P].rearrange("p (h q) -> p h q", h=NH)
        c_hi, c_lo = spr_lo[0:NH, 0:S], spr_lo[0:NH, S:2 * S]
        x2 = [ring[:, 10 * SLOT + t * D:10 * SLOT + (t + 1) * D] for t in range(TT)]
        tn = [qk2[:, i, :] for i in (0, 1, 4, 5)]
        tT = [slot(4 + h).rearrange("p (k t) -> p k t", k=4) for h in range(2)]
        ohslot = qk[:, 4:8, :].rearrange("p a t -> p (a t)").rearrange("p (a n) -> p a n", n=P)
        lgT = qk[0:E, 4, :]
        payload = qk[:, 8:11, :].rearrange("p a t -> p (a t)")[:, 0:16 * 2 * ITEMS].rearrange(
            "p (a c n) -> p a c n", a=16, c=2)
        b1raw = slot(7)[0:64, :]
        b2raw = slot(3)[0:64, 0:D]
        g2b = slot(6)[:, 0:D]
        small = slot(6)[:, D:2 * D]
        gath = qk2[:, 0, :]
        glu = qk2[:, 1, :]
        lin = qk2[:, 2, :]
        sig = qk2[:, 3, :]
        yout = qk2[:, 4, :]
        gfb = qk2[:, 5, :]
        rt = qk[:, 12:16, :].rearrange("p a t -> p (a t)")

        bank = [ctx.enter_context(nc.psum_tensor(f"bank{i}", [P, BANK], F32)) for i in range(8)]

        sbank = [bank[i] for i in (0, 1, 2, 4)]

        ss1, rs1, r1 = cols[:, 0:4], cols[:, 4:8], cols[:, 8:12]
        negmax, rsum, rinv = cols[:, 12:14], cols[:, 14:16], cols[:, 16:18]
        gmix = cols[:, 18:26]
        rsm, rm = cols[:, 34:42], cols[:, 42:50]
        ss2, rs2, r2 = cols[:, 50:54], cols[:, 54:58], cols[:, 58:62]
        pmod = cols[0:64, 62:63]
        bfc = cols[0:NH, 63:64]
        ss3, rs3, r3 = cols[:, 64:68], cols[:, 68:72], cols[:, 72:76]
        row1 = cols[:, 76:92]
        epsc = cols[:, 92:93]
        smax = cols[:, 93:95]
        wfraw = sb("wfraw", [P, KT, NH])
        wfr = sb("wfr", [P, 2, KT * NH], F32R)
        wrt = small[:, 0:KT * E].rearrange("p (k e) -> p k e", k=KT)
        brb = small[:, 256:256 + E]
        wrg = small[:, 288:288 + KT * E].rearrange("p (k e) -> p k e", k=KT)
        chosen = small[:, 544:608].bitcast(BF16)
        g2col = cols[:, 96:104]

        full = [sem(f"slot{z}_full") for z in range(SLOTS)]
        x_in = [sem(f"x_in{t}") for t in range(TT)]
        g1_in, vec_in, wrt_in = sem("g1_in"), sem("vec_in"), sem("wrt_in")
        g2_in, bias_in, gf_in = sem("g2_in"), sem("bias_in"), sem("gf_in")
        consts = sem("consts")
        split_hi, split_lo = sem("split_hi"), sem("split_lo")
        used = sem("pieces_used")
        h_sq, h_rs, h_norm, h_turned, h_hi, h_lo = (sem(n) for n in ("h_sq", "h_rs", "h_norm", "h_turned", "h_hi", "h_lo"))
        qk_copied, v_copied = sem("qk_copied"), sem("v_copied")
        f_split, f_mm, f_steps, c_split = sem("f_split"), sem("f_mm"), sem("f_steps"), sem("c_split")
        s_ready, neg_ready, p_ready, ps_ready = sem("s_ready"), sem("neg_ready"), sem("p_ready"), sem("ps_ready")
        pt_turned, pt_ready, pvf_done = sem("pt_turned"), sem("pt_ready"), sem("pvf_done")
        z_ready, absz, ln_ready, sp_ready = sem("z_ready"), sem("absz"), sem("ln_ready"), sem("sp_ready")
        e_ready, sp_raw = sem("e_ready"), sem("sp_raw")
        loga_ready, a_ready, pvs_done = sem("loga_ready"), sem("a_ready"), sem("pvs_done")
        mix_hi, mix_sq, mix_lo = sem("mix_hi"), sem("mix_sq"), sem("mix_lo")
        o_copied, mixs_hi, mixs_lo, mixs_sq = (sem(n) for n in ("o_copied", "mixs_hi", "mixs_lo", "mixs_sq"))
        tri_ready = sem("tri_ready")
        ssm_done, oproj, x2_add = sem("ssm_done"), sem("oproj"), sem("x2_add")
        sq_summed, stage_left = sem("sq_summed"), sem("stage_left")
        rsm_ready, ms_read = sem("rsm_ready"), sem("ms_read")
        x2_in, x2_sq, x2_rs, tn_ready = sem("x2_in"), sem("x2_sq"), sem("x2_rs"), sem("tn_ready")
        r2_ready = sem("r2_ready")
        x2_out, tn_out = sem("x2_out"), sem("tn_out")
        x2_turned, tT_copied, logits_done, lgT_done, lgT_copied = (sem(n) for n in ("x2_turned", "tT_copied", "logits_done", "lgT_done", "lgT_copied"))
        wrg_ready = sem("wrg_ready")
        exp4, onehots, counted, slots_ready, tab_mm, tables = (sem(n) for n in ("exp4", "onehots", "counted", "slots_ready", "tab_mm", "tables"))
        bias_hi, bias_lo = sem("bias_hi"), sem("bias_lo")
        gath_zero = sem("gath_zero")
        idx_copied, gathered, x_turned, xT_hi_r, xT_lo_r = (sem(n) for n in ("idx_copied", "gathered", "x_turned", "xT_hi_ready", "xT_lo_ready"))
        sel1_r, sel2_r, sel1_used, clipped, sig_done, act_made = (sem(n) for n in ("sel1_ready", "sel2_ready", "bias1_added", "clipped", "sig_done", "act_made"))
        gs_made, weight_ready = sem("gs_made"), sem("weight_ready")
        a_turned, aT_hi_r, aT_lo_r, y_ready = (sem(n) for n in ("a_turned", "aT_hi_ready", "aT_lo_ready", "y_ready"))
        sidx_copied, scattered, all_scattered, yout_free = (sem(n) for n in ("sidx_copied", "scattered", "all_scattered", "yout_free"))
        fin_sum, fin_sq, fin_rs, fin_ready, out_done = (sem(n) for n in ("fin_sum", "fin_sq", "fin_rs", "fin_ready", "out_done"))
        fin_in = [[sem(f"fin_in{t}_{j}") for j in range(TOPK + 1)] for t in range(TT)]
        fin_again = sem("fin_again")
        steps = {n: sem(n + "_steps") for n in ("pool", "dve")}
        count = {n: 0 for n in steps}

        def wait(eng, semaphore, value):
            if not (isinstance(value, int) and value == 0):
                eng.wait_ge(semaphore, value)

        def link(eng, name, ins):
            count[name] += 1
            ins.then_inc(steps[name], 1)
            eng.wait_ge(steps[name], count[name])

        def piece_ap(g):
            if g < W_IN_PIECES:
                return ring[:, g * PIECE:(g + 1) * PIECE]
            h = g - W_IN_PIECES
            return ring[:, 6 * SLOT + h * PIECE:6 * SLOT + (h + 1) * PIECE]

        def moe_slot(c):
            return c % SLOTS

        def loads_before(z):
            return 2 if 6 <= z < 10 else 1

        class Run:
            def __init__(self, first, n, base):
                self.first, self.n, self.base = first, n, base
                self.turn0 = (base - MOE0) // (2 * SLOTS)
                self.used0 = base - OPROJ_PIECES
                self.split0 = MOE0 + first * SPLIT

            def split(self, r, j):
                return r * SPLIT + (self.split0 - W2P + before_piece(j + 1))

            def freed(self, r, c):
                if c == WHOLE // 2:
                    return used, r * (W1P + W2P) + (self.used0 - W2P + WHOLE + 2)
                return split_lo, self.split(r, 2 * c + 1)

            def freed_first(self, c):
                if c == WHOLE // 2:
                    return used, self.used0 + WHOLE + 2
                return split_lo, self.split0 + 2 * c + 2

        MAIN = Run(0, E, MOE0)
        REST = Run(E, OVER, MOE0 + E * (W1P + W2P))

        block = ctx.enter_context(nc.Block())

        @block.sync
        def _(sp):
            for t in range(TT):
                sp.dma_start(xs[t], x_d[t * P:(t + 1) * P, :]).then_inc(x_in[t], 16)
                if t == 0:
                    sp.dma_start(g1b, norm1_g[0:1, :].partition_broadcast(P)).then_inc(g1_in, 16)
            for z in range(SLOTS):
                group, half = z // 2, z % 2
                c0 = (3 * HW + NH + group * HW) if group < 3 else (group - 3) * HW
                sp.dma_start(slot(z).rearrange("p (k n) -> p k n", k=4),
                             w_in_d.rearrange("(k p) n -> p k n", p=P)[:, 4 * half:4 * half + 4, c0:c0 + HW]
                             ).then_inc(full[z], 16)
            for z in range(6, 10):
                k = (2 * (z - 6) + 4) % KT
                sp.wait_ge(split_lo, 2 * z + 2)
                sp.dma_start(slot(z).rearrange("p (k n) -> p k n", k=2),
                             w_out_d.rearrange("(k p) n -> p k n", p=P)[:, k:k + 2, :]).then_inc(full[z], 16)

            def load_w1(e, k, z):
                sp.dma_start(slot(z), w1_d[e, k]).then_inc(full[z], 16)

            sp.wait_ge(split_lo, W_IN_PIECES)
            for t in range(TT):
                sp.dma_start(x2[t], x_d[t * P:(t + 1) * P, :]).then_inc(x2_in, 16)
            sp.wait_ge(split_lo, W_IN_PIECES + 2)
            sp.dma_start(wrt, w_router_d.rearrange("(k p) e -> p k e", p=P)).then_inc(wrt_in, 16)
            sp.dma_start(brb, b_router[0:1, :].partition_broadcast(P)).then_inc(wrt_in, 16)
            sp.dma_start(g2b, norm2_g[0:1, :].partition_broadcast(P)).then_inc(g2_in, 16)
            sp.wait_ge(split_lo, W_IN_PIECES + 4)
            for h in range(2):
                sp.dma_start(b1raw[32 * h:32 * h + 32, :], b1[0]).then_inc(bias_in, 16)
            sp.wait_ge(mix_sq, NH)
            for h in range(2):
                sp.dma_start(b2raw[32 * h:32 * h + 32, :], b2[0]).then_inc(bias_in, 16)
            for c in range(3):
                load_w1(0, c, moe_slot(c))
            sp.wait_ge(bias_lo, 2)
            for c in (3, 7):
                load_w1(0, c, moe_slot(c))

            def load_body(e_w1, e_w2, c, waits):
                z = (c + 8) % SLOTS
                if waits is not None:
                    sp.wait_ge(*waits)
                if c < KT:
                    src = w1_d[e_w1, c] if isinstance(e_w1, int) else \
                        w1_d[bass.ds(e_w1, 1), c].rearrange("e p n -> p (e n)")
                    sp.dma_start(slot(z), src).then_inc(full[z], 16)
                else:
                    k = 2 * (c - KT)
                    src = w2_d[e_w2, k:k + 2].rearrange("k p n -> p k n") if isinstance(e_w2, int) else \
                        w2_d[bass.ds(e_w2, 1), k:k + 2].rearrange("e k p n -> p (e k) n")
                    sp.dma_start(slot(z).rearrange("p (k n) -> p k n", k=2), src).then_inc(full[z], 16)

            for c in range(SLOTS):
                if c == 2:
                    for t in range(TT):
                        sp.wait_ge(tn_ready, t + 1)
                        sp.dma_start(tn_d[t * P:(t + 1) * P, :], tn[t]).then_inc(tn_out, 16)
                        sp.dma_start(x2_d[t * P:(t + 1) * P, :], x2[t]).then_inc(x2_out, 16)
                    sp.wait_ge(logits_done, 1)
                    for k in (4, 5):
                        load_w1(0, k, moe_slot(k))
                    sp.wait_ge(x2_out, 16 * TT)
                    sp.wait_ge(x2_turned, 2 * TT)
                if c == 4:
                    sp.wait_ge(gathered, 16)
                    load_w1(0, 6, moe_slot(6))
                    sp.dma_start(gfb, norm_f_g.rearrange("(a d) -> a d", a=1).partition_broadcast(P)).then_inc(gf_in, 16)
                load_body(1, 0, c, (split_lo, MOE0) if c < 4 else MAIN.freed_first(c - 4))
            with sp.Fori(2, E) as t:
                for c in range(SLOTS):
                    load_body(t, t - 1, c, MAIN.freed(t - 1, c))
            for c in range(KT, SLOTS):
                sp.wait_ge(*MAIN.freed(E - 1, c - KT))
                z = moe_slot(12 * E - 4 + c - KT)
                k = 2 * (c - KT)
                sp.dma_start(slot(z).rearrange("p (k n) -> p k n", k=2),
                             w2_d[E - 1, k:k + 2].rearrange("k p n -> p k n")).then_inc(full[z], 16)

            def load_residual(signals):
                for t in range(TT):
                    sp.dma_start(ring[:, t * 5 * D:t * 5 * D + D], x2_d[t * P:(t + 1) * P, :]).then_inc(signals[t], 16)

            for c in range(4, SLOTS):
                sp.wait_ge(*MAIN.freed(E - 1, c))
            load_residual([s[0] for s in fin_in])

            sp.wait_ge(tables, 1)
            n_over = sp.value_load(novi[0:1, 0:1], min_val=0, max_val=OVER)
            with sp.If(n_over > 0):
                def expert(i):
                    return sp.value_load(eidtab[0:1, bass.ds(i, 1)] if not isinstance(i, int) else
                                         eidtab[0:1, i:i + 1], min_val=0, max_val=E - 1)
                for t in range(TT):
                    sp.wait_ge(fin_in[t][0], 16)
                e0 = expert(0)
                for c in range(KT):
                    z = moe_slot(c)
                    sp.wait_ge(*MAIN.freed(E - 1, c + 4))
                    sp.dma_start(slot(z), w1_d[bass.ds(e0, 1), c].rearrange("e p n -> p (e n)")).then_inc(full[z], 16)
                ew1, ew2 = expert(1), expert(0)
                for c in range(SLOTS):
                    load_body(ew1, ew2, c, REST.freed(0, c) if c < 4 else REST.freed_first(c - 4))
                with sp.Fori(2, OVER) as t:
                    ew1, ew2 = expert(t), expert(t - 1)
                    for c in range(SLOTS):
                        load_body(ew1, ew2, c, REST.freed(t - 1, c))
                el = expert(OVER - 1)
                for c in range(KT, SLOTS):
                    z = moe_slot((24 * OVER - 8) // 2 + c - KT)
                    k = 2 * (c - KT)
                    sp.wait_ge(*REST.freed(OVER - 1, c - KT))
                    sp.dma_start(slot(z).rearrange("p (k n) -> p k n", k=2),
                                 w2_d[bass.ds(el, 1), k:k + 2].rearrange("e k p n -> p (e k) n")).then_inc(full[z], 16)

                for c in range(4, SLOTS):
                    sp.wait_ge(*REST.freed(OVER - 1, c))
                load_residual([fin_again] * TT)

            sp.wait_ge(all_scattered, 1)
            for t in range(TT):
                o = t * 5 * D
                for j in range(TOPK):
                    sp.dma_start(ring[:, o + (j + 1) * D:o + (j + 2) * D],
                                 y_d.rearrange("(t j) d -> t j d", j=TOPK)[t * P:(t + 1) * P, j, :]).then_inc(fin_in[t][j + 1], 16)
            for t in range(TT):
                sp.wait_ge(fin_ready, t + 1)
                sp.dma_start(out_d[t * P:(t + 1) * P, :], ring[:, t * 5 * D:t * 5 * D + D]).then_inc(out_done, 16)
            sp.wait_ge(out_done, 16 * TT)
            sp.wait_ge(tn_out, 16 * TT)

        @block.gpsimd
        def _(pool):
            pool.dma_start(wfraw[:], w_in_d.rearrange("(k p) n -> p k n", p=P)[:, :, 3 * HW:3 * HW + NH]).then_inc(vec_in, 16)
            pool.dma_start(bfc, b_f.rearrange("a h -> h a"), allow_slow_non_contiguous=True).then_inc(vec_in, 16)
            pool.dma_start(gmix[:, 0:4], g_fox[0].rearrange("(c p) -> p c", p=P), allow_slow_non_contiguous=True).then_inc(vec_in, 16)
            pool.dma_start(g2col, norm2_g[0].rearrange("(c p) -> p c", p=P), allow_slow_non_contiguous=True).then_inc(vec_in, 16)
            pool.dma_start(gmix[:, 4:8], g_sb[0].rearrange("(c p) -> p c", p=P), allow_slow_non_contiguous=True).then_inc(vec_in, 16)

            def fill(ap, value):
                link(pool, "pool", nc.gpsimd.memset(ap, value))

            def choose(ap, pattern, op, fill_value, base, mult):
                return nc.gpsimd.affine_select(out=ap, in_=ap, pattern=pattern, compare_op=op, fill=fill_value,
                                               base=base, channel_multiplier=mult)
            made = [0]

            def constant(ins):
                made[0] += 1
                ins.then_inc(consts, 1)
                pool.wait_ge(consts, made[0])

            def count_up(ap, pattern, base, mult):
                return nc.gpsimd.iota(ap, pattern, base=base, channel_multiplier=mult,
                                      allow_small_or_imprecise_dtypes=True)
            fill(identF[:], 0.0)
            constant(choose(identF[:], [[-1, P]], ALU.not_equal, 1.0, 0, 1))
            constant(nc.gpsimd.memset(epsc, EPS))
            fill(identB[:], 0.0)
            constant(choose(identB[:], [[-1, P]], ALU.not_equal, 1.0, 0, 1))
            fill(maskF, 0.0)
            constant(choose(maskF, [[-1, P]], ALU.is_ge, MASKED, 0, 1))
            fill(maskS, 0.0)
            constant(choose(maskS, [[1, P]], ALU.is_gt, MASKED, 0, -1))
            fill(before[:], 1.0)
            constant(choose(before[:], [[1, P]], ALU.is_gt, 0.0, 0, -1))
            constant(nc.gpsimd.memset(ones[:], 1.0))
            constant(nc.gpsimd.memset(onesB[:], 1.0))
            constant(count_up(iotas[:], [[1, P]], 0, 0))
            constant(count_up(cols[0:32, 62:63], [[0, 1]], 0, 1))
            constant(count_up(cols[32:64, 62:63], [[0, 1]], 0, 1))
            constant(count_up(row1, [[TOPK * P, TT], [1, TOPK]], 1, TOPK))
            pool.wait_ge(split_lo, 10)
            fill(tri_raw, -1.0)
            constant(choose(tri_raw, [[-1, P]], ALU.is_ge, 0.0, 0, 1))
            constant(nc.gpsimd.memset(one_raw, -1.0))
            fill(sel8, 0.0)
            constant(choose(sel8, [[-1, NH], [0, P]], ALU.not_equal, 1.0, 0, 1))

            bound, zero = pool.alloc_register("bound"), pool.alloc_register("nought")
            pool.reg_mov(zero, 0)

            def gather(i):
                if not (isinstance(i, int) and i == 0):
                    pool.wait_ge(x_turned, i)
                nc.gpsimd.tensor_copy(gidx[:], gtab[:, i:i + 1] if isinstance(i, int) else gtab[:, bass.ds(i, 1)]
                                      ).then_inc(idx_copied, 1)
                pool.wait_ge(idx_copied, i + 1)
                pool.reg_add(bound, zero, S - 1)
                nc.gpsimd.indirect_dma_start(out=gath, out_offset=None, in_=tn_d[:, :],
                                             in_offset=bass.IndirectOffsetOnAxis(ap=gidx[:, 0:1], axis=0),
                                             bounds_check=bound, oob_is_err=False).then_inc(gathered, 16)

            def scatter(i):
                pool.wait_ge(y_ready, i + 1)
                nc.gpsimd.tensor_copy(sidx[:], stab[:, i:i + 1] if isinstance(i, int) else stab[:, bass.ds(i, 1)]
                                      ).then_inc(sidx_copied, 1)
                pool.wait_ge(sidx_copied, i + 1)
                pool.reg_add(bound, zero, S * TOPK - 1)
                nc.gpsimd.indirect_dma_start(out=y_d[:, :], out_offset=bass.IndirectOffsetOnAxis(ap=sidx[:, 0:1], axis=0),
                                             in_=yout, in_offset=None,
                                             bounds_check=bound, oob_is_err=False).then_inc(scattered, 16)
                pool.wait_ge(scattered, i * 16 + 16)
                pool.sem_inc(yout_free, 1)

            pool.wait_ge(tn_out, 16 * TT)
            nc.gpsimd.memset(gath, 0.0).then_inc(gath_zero, 1)
            pool.sem_inc(yout_free, 1)
            pool.wait_ge(gath_zero, 1)
            pool.wait_ge(tables, 1)
            for i in range(3):
                gather(i)
            with pool.Fori(2, E - 1) as i:
                scatter(i - 2)
                gather(i + 1)
            for i in range(E - 3, E):
                scatter(i)
            n_over = pool.value_load(novi[0:1, 0:1], min_val=0, max_val=OVER)
            with pool.If(n_over > 0):
                gather(E)
                gather(E + 1)
                with pool.Fori(E + 1, ITEMS - 1) as i:
                    gather(i + 1)
                    scatter(i - 1)
                for i in range(ITEMS - 2, ITEMS):
                    scatter(i)
            nc.gpsimd.memset(gidx[:], 0).then_inc(all_scattered, 1)

        @block.scalar
        def _(act):
            def hi(dst, src, wait_full, wait_used):
                if wait_full is not None:
                    act.wait_ge(*wait_full)
                if wait_used is not None:
                    act.wait_ge(used, wait_used)
                nc.scalar.copy(dst, src).then_inc(split_hi, 1)

            def hi_early(g):
                z = g // 2 if g < W_IN_PIECES else 6 + (g - W_IN_PIECES) // 2
                hi(stage_hi[:, g % STAGES, :], piece_ap(g),
                   (full[z], 16 if g < W_IN_PIECES else 32) if g % 2 == 0 else None,
                   g - STAGES + 1 if STAGES <= g < W_IN_PIECES + STAGES else None)

            act.wait_ge(consts, 2)
            for t in range(TT):
                act.wait_ge(x_in[t], 16)
                nc.scalar.activation(sqjunk, xs[t], ACT.Square, accum_out=ss1[:, t:t + 1]).then_inc(h_sq, 1)
                act.wait_ge(h_sq, t + 1)
                nc.scalar.activation(rs1[:, t:t + 1], ss1[:, t:t + 1], ACT.Sqrt, scale=1.0 / D, bias=epsc).then_inc(h_rs, 1)
            for j in range(2 * TT):
                t, h = j // 2, j % 2
                act.wait_ge(h_turned, j + 1)
                nc.scalar.copy(hT_hi[:, 4 * h:4 * h + 4, t * P:(t + 1) * P],
                               bank[4 + j % 4][:].rearrange("p (k t) -> p k t", k=4)).then_inc(h_hi, 1)
                if j == 3:
                    for g in range(STAGES):
                        hi_early(g)

            def qk_evac(group):
                tile0 = {0: 8, 1: 12, 3: 0, 4: 4}[group]
                b0 = 0 if group == 0 else 4
                act.wait_ge(used, 4 * group + 4)
                for c in range(4):
                    nc.scalar.activation(qk[:, tile0 + c, :], bank[b0 + c][:], ACT.Copy,
                                         scale=HD ** -0.5 if group in (0, 3) else 1.0).then_inc(qk_copied, 1)

            for group in range(2):
                for g in range(4 * (group + 1), 4 * (group + 2)):
                    hi_early(g)
                qk_evac(group)
            for g in range(12, 16):
                hi_early(g)
            act.wait_ge(vec_in, 80)
            nc.scalar.copy(wfr[:, 0, :], wfraw[:].rearrange("p k h -> p (k h)")).then_inc(f_split, 1)
            nc.scalar.preload_act_table_set("natural_log_exp_and_others")
            def forget_gate():
                act.wait_ge(f_steps, 2)
                nc.scalar.activation(negc, negc, ACT.Exp).then_inc(f_steps, 1)
                act.wait_ge(f_steps, 3)
                nc.scalar.activation(negc, negc, ACT.Ln, bias=1.0).then_inc(f_steps, 1)

            def sb_exp(u):
                n = (u % TT + 1) * P
                act.wait_ge(loga_ready, u + 1)
                if u >= 2:
                    act.wait_ge(pvs_done, u - 1)
                nc.scalar.activation(abuf[:, u % 2, 0:n], bank[u % 3][:, 0:n], ACT.Exp).then_inc(a_ready, 1)

            def copy_o(n):
                half = slice(64 * (n % 2), 64 * (n % 2) + 64)
                act.wait_ge(pvs_done, TT * (n + 1))
                nc.scalar.copy(qk[half, 8 + n // 2, :], bank[3][half, :]).then_inc(o_copied, 1)

            def mix_evac(n):
                half = slice(64 * (n % 2), 64 * (n % 2) + 64)
                c = n // 2
                act.wait_ge(pvf_done, TT * (n + 1))
                nc.scalar.activation(hT_hi[half, c, :], bank[3][half, :], ACT.Copy, scale=gmix[half, c:c + 1]).then_inc(mix_hi, 1)
                nc.scalar.activation(qk[half, c, :], bank[3][half, :], ACT.Square).then_inc(mix_sq, 1)

            for u in range(UNITS + 3):
                if u < UNITS:
                    n = (u % TT + 1) * P
                    act.wait_ge(z_ready, u + 1)
                    if u >= 2:
                        act.wait_ge(sp_raw, u - 1)
                    nc.scalar.activation(lbuf[:, u % 2, 0:n], bank[u % 3][:, 0:n], ACT.Abs).then_inc(absz, 1)
                    act.wait_ge(absz, u + 1)
                    nc.scalar.activation(lbuf[:, u % 2, 0:n], lbuf[:, u % 2, 0:n], ACT.Exp, scale=-1.0).then_inc(e_ready, 1)
                    act.wait_ge(e_ready, u + 1)
                    nc.scalar.activation(lbuf[:, u % 2, 0:n], lbuf[:, u % 2, 0:n], ACT.Ln, bias=1.0).then_inc(ln_ready, 1)
                if u == 4:
                    forget_gate()
                if u == fill_at(31):
                    qk_evac(3)
                if u == fill_at(63):
                    qk_evac(4)
                if 2 <= u < UNITS + 2:
                    sb_exp(u - 2)
                if u >= 6 and (u - 6) % TT == 0:
                    copy_o((u - 6) // TT)
                for g in range(16, W_IN_PIECES):
                    if split_at(g) == u:
                        hi_early(g)
            def stick_mix(c):
                if c == 0:
                    act.wait_ge(o_copied, NH)
                    act.wait_ge(used, W_IN_PIECES)
                nc.scalar.activation(hT_hi[:, 4 + c, :], qk[:, 8 + c, :], ACT.Copy, scale=gmix[:, 4 + c:5 + c]).then_inc(mixs_hi, 1)
                nc.scalar.activation(qk[:, 12 + c, :], qk[:, 8 + c, :], ACT.Square).then_inc(mixs_sq, 1)

            def scale_of_norm(kind):
                cs = slice(4 * kind, 4 * kind + 4)
                act.wait_ge(ssm_done, 2 - kind)
                nc.scalar.activation(rsm[:, cs], bank[7][:, cs], ACT.Ln, scale=1.0 / HW, bias=epsc).then_inc(ms_read, 1)
                act.wait_ge(ms_read, 2 - kind)
                nc.scalar.activation(rm[:, cs], rsm[:, cs], ACT.Exp, scale=-0.5).then_inc(rsm_ready, 1)

            for u in range(UNITS + 4):
                if u < UNITS:
                    n = (u % TT + 1) * P
                    act.wait_ge(neg_ready, u + 1)
                    if u >= 4:
                        act.wait_ge(pt_turned, u - 3)
                    nc.scalar.activation(pbuf[:, u % 4, 0:n], sbank[u % 4][:, 0:n], ACT.Exp,
                                         bias=negmax[:, u % 2:u % 2 + 1],
                                         accum_out=rsum[:, u % 2:u % 2 + 1]).then_inc(p_ready, 1)
                if u < 4:
                    stick_mix(u)
                    hi_early(W_IN_PIECES + u)
                if u == 7:
                    scale_of_norm(1)
                if u >= 7 and (u - 7) % TT == 0:
                    mix_evac((u - 7) // TT)
                if u > UNITS:
                    act.wait_ge(stage_left, u - UNITS)
                    hi_early(W_IN_PIECES + 4 + u - UNITS - 1)
            act.wait_ge(oproj, 8)
            hi_early(MOE0 - 1)
            scale_of_norm(0)
            act.wait_ge(bias_in, 64)
            nc.scalar.copy(bias1, b1raw).then_inc(bias_hi, 1)
            nc.scalar.copy(bias2, b2raw).then_inc(bias_hi, 1)
            nc.scalar.preload_act_table_set("sqrt_and_others")
            for t in range(TT):
                for h in range(2):
                    act.wait_ge(x2_turned, 2 * t + h + 1)
                    nc.scalar.copy(tT[h][:, :, t * P:(t + 1) * P], bank[2 * t + h][:].rearrange("p (k t) -> p k t", k=4)).then_inc(tT_copied, 1)
                act.wait_ge(x2_add, 2 * TT + 2 * t + 2)
                nc.scalar.activation(tn[t], x2[t], ACT.Square, accum_out=ss2[:, t:t + 1]).then_inc(x2_sq, 1)
                act.wait_ge(x2_sq, t + 1)
                nc.scalar.activation(rs2[:, t:t + 1], ss2[:, t:t + 1], ACT.Sqrt, scale=1.0 / D, bias=epsc).then_inc(x2_rs, 1)
                act.wait_ge(lgT_done, t + 1)
                nc.scalar.copy(lgT[:, t * P:(t + 1) * P], bank[0][0:E, t * P:(t + 1) * P]).then_inc(lgT_copied, 1)
            nc.scalar.preload_act_table_set("natural_log_exp_and_others")
            act.wait_ge(exp4, 1)
            nc.scalar.activation(rt[:, 0:16], rt[:, 0:16], ACT.Exp).then_inc(exp4, 1)
            nc.scalar.preload_act_table_set("sigmoid_and_others")

            def hi_moe(j, z, turns, used_at):
                h = j % 2
                hi(stage_hi[:, j % STAGES, :], slot(z)[:, h * PIECE:(h + 1) * PIECE],
                   (full[z], turns) if h == 0 else None, used_at)

            def x_evac(t):
                act.wait_ge(x_turned, t + 1)
                nc.scalar.copy(xT_hi[:, 0:4, :], bank[6][:].rearrange("p (k t) -> p k t", k=4)).then_inc(xT_hi_r, 1)
                nc.scalar.copy(xT_7, bank[7][:, 3 * P:4 * P])
                nc.scalar.copy(xT_hi[:, 4:7, :], bank[7][:, 0:3 * P].rearrange("p (k t) -> p k t", k=3)).then_inc(xT_hi_r, 1)

            def a_evac(t):
                act.wait_ge(a_turned, t + 1)
                for h in range(2):
                    nc.scalar.copy(aT_hi[:, 4 * h:4 * h + 4, :], bank[6 + h][:].rearrange("p (k t) -> p k t", k=4)).then_inc(aT_hi_r, 1)

            def sigmoid(t):
                act.wait_ge(clipped, 2 * t + 1)
                wait(act, act_made, t)
                nc.scalar.activation(sig, glu, ACT.Sigmoid, scale=ALPHA).then_inc(sig_done, 1)

            def y_evac(t, used_at):
                act.wait_ge(used, used_at)
                act.wait_ge(yout_free, t + 1)
                act.wait_ge(weight_ready, t + 1)
                for h in range(2):
                    ins = nc.scalar.activation(yout[:, h * BANK:(h + 1) * BANK], bank[4 + h][:], ACT.Copy,
                                               scale=wcol[:])
                ins.then_inc(y_ready, 1)

            def run_items(run):
                q0, n, b, T0 = run.first, run.n, run.base, run.turn0
                ub = b - OPROJ_PIECES

                def turns(z, k):
                    return 16 * (loads_before(z) + k)

                for j in range(W1P):
                    if j == STAGES:
                        x_evac(q0)
                    if j >= WHOLE:
                        continue
                    z = moe_slot(j // 2)
                    if b == MOE0 and j < STAGES:
                        hi_moe(j, z, turns(z, T0 + 1), None)
                    else:
                        hi_moe(j, z, turns(z, T0 + 1), ub + j - STAGES + 1)
                sigmoid(q0)
                x_evac(q0 + 1)

                def body(r, first=False, last=False):
                    t = r + q0
                    for j in range(W1P + W2P):
                        s = j // 2
                        z = (s + 8) % SLOTS
                        k = T0 if s < 4 else T0 + 1
                        free = j - STAGES if j - STAGES not in (WHOLE, WHOLE + 1) else j - 2 * STAGES
                        if j not in (WHOLE, WHOLE + 1):
                            hi_moe(j, z, r * 16 + turns(z, k), r * 24 + (ub - 8 + free + 1))
                        if j == 3 and not first:
                            y_evac(t - 2, r * 24 + (ub - 8))
                        if j == 12:
                            a_evac(t - 1)
                        if j == 19:
                            sigmoid(t)
                        if j == 21 and not last:
                            x_evac(t + 1)
                body(1, first=True)
                with act.Fori(2, n - 1) as r:
                    body(r)
                body(n - 1, last=True)
                y_evac(q0 + n - 2, ub + 24 * n - 8)
                a_evac(q0 + n - 1)
                for j in range(W2P):
                    c = (24 * n - 8) // 2 + j // 2
                    z = moe_slot(c)
                    hi_moe(j, z, turns(z, T0 + c // SLOTS + 1), ub + 24 * n - 8 + j - STAGES + 1)
                y_evac(q0 + n - 1, ub + 24 * n)

            run_items(MAIN)
            act.wait_ge(tables, 1)
            n_over = act.value_load(novi[0:1, 0:1], min_val=0, max_val=OVER)
            with act.If(n_over > 0):
                run_items(REST)
            for t in range(TT):
                act.wait_ge(fin_sum, t * 4 + 4)
                nc.scalar.activation(ring[:, t * 5 * D + D:t * 5 * D + 2 * D], ring[:, t * 5 * D:t * 5 * D + D],
                                     ACT.Square, accum_out=ss3[:, t:t + 1]).then_inc(fin_sq, 1)
                act.wait_ge(fin_sq, t + 1)
                nc.scalar.activation(rs3[:, t:t + 1], ss3[:, t:t + 1], ACT.Sqrt, scale=1.0 / D, bias=epsc).then_inc(fin_rs, 1)

        @block.vector
        def _(dve):
            def chained(ins):
                link(dve, "dve", ins)

            def loose(ins):
                count["dve"] += 1
                ins.then_inc(steps["dve"], 1)

            def lo(dst, src, hi_ap, g1):
                dve.wait_ge(split_hi, g1)
                nc.vector.tensor_tensor(dst, src, hi_ap.bitcast(F32), ALU.subtract).then_inc(split_lo, 1)

            def lo_early(g):
                lo(stage_lo[:, g % STAGES, :], piece_ap(g), stage_hi[:, g % STAGES, :], g + 1)

            dve.wait_ge(g1_in, 16)
            for t in range(TT):
                dve.wait_ge(h_rs, t + 1)
                chained(nc.vector.reciprocal(r1[:, t:t + 1], rs1[:, t:t + 1]))
                nc.vector.scalar_tensor_tensor(out=xs[t], in0=xs[t], scalar=r1[:, t:t + 1], in1=g1b,
                                               op0=ALU.mult, op1=ALU.mult).then_inc(h_norm, 1)
            for j in range(2 * TT):
                t, h = j // 2, j % 2
                dve.wait_ge(h_hi, j + 1)
                a = (slice(None), slice(4 * h, 4 * h + 4), slice(t * P, (t + 1) * P))
                nc.vector.tensor_tensor(hT_lo[a], bank[4 + j % 4][:].rearrange("p (k t) -> p k t", k=4),
                                        hT_hi[a].bitcast(F32), ALU.subtract).then_inc(h_lo, 1)
                if j == 3:
                    for g in range(STAGES):
                        lo_early(g)

            def v_evac(group):
                dve.wait_ge(used, 4 * group + 4)
                for t in range(TT):
                    o = HW if group == 2 else 0
                    b0 = 0 if group == 2 else 4
                    nc.vector.tensor_copy(vbuf[:, t, o:o + HW], bank[b0 + t][:]).then_inc(v_copied, 1)

            for g in range(STAGES, 12):
                lo_early(g)
            dve.wait_ge(consts, 15)
            nc.vector.tensor_copy(neg_tri[:], tri_raw).then_inc(tri_ready, 1)
            nc.vector.tensor_copy(neg_one[:], one_raw).then_inc(tri_ready, 1)
            for g in range(12, 15):
                lo_early(g)
            dve.wait_ge(f_split, 1)
            nc.vector.tensor_tensor(wfr[:, 1, :], wfraw[:].rearrange("p k h -> p (k h)"), wfr[:, 0, :].bitcast(F32),
                                    ALU.subtract).then_inc(f_split, 1)
            v_evac(2)
            lo_early(15)
            fu, m = csum, fmax

            def forget_gate(part):
                if part == 0:
                    dve.wait_ge(f_mm, 1)
                    dve.wait_ge(consts, 15)
                    nc.vector.tensor_scalar(fu, bank[3][0:NH, :], bfc, None, ALU.add).then_inc(f_steps, 1)
                    dve.wait_ge(f_steps, 1)
                    nc.vector.scalar_tensor_tensor(out=negc, in0=fu, scalar=-1.0, in1=fu, op0=ALU.mult, op1=ALU.min).then_inc(f_steps, 1)
                    chained(nc.vector.tensor_scalar(m, fu, -1.0, 0.0, ALU.mult, ALU.max))
                else:
                    dve.wait_ge(f_steps, 4)
                    chained(nc.vector.tensor_tensor_scan(fu, m, negc, 0.0, ALU.add, ALU.add))

            def sp_cols(u):
                i = u % TT
                return slice(P * i * (i + 1) // 2, P * (i + 1) * (i + 2) // 2)

            for u in range(UNITS + 3):
                if 1 <= u <= UNITS:
                    v = u - 1
                    n = (v % TT + 1) * P
                    dve.wait_ge(ln_ready, v + 1)
                    if v >= 2:
                        dve.wait_ge(sp_ready, v - 1)
                    elif v == 0:
                        dve.wait_ge(tri_ready, 2)
                    nc.vector.scalar_tensor_tensor(out=spraw[:, v % 2, 0:n], in0=bank[v % 3][:, 0:n], scalar=0.0,
                                                   in1=lbuf[:, v % 2, 0:n], op0=ALU.max, op1=ALU.add).then_inc(sp_raw, 1)
                    dve.wait_ge(sp_raw, v + 1)
                    if v >= TT:
                        dve.wait_ge(loga_ready, TT * (v // TT))
                    chained(nc.vector.tensor_copy(spr_hi[:, sp_cols(v)], spraw[:, v % 2, 0:n]))
                    nc.vector.tensor_tensor(spr_lo[:, sp_cols(v)], spraw[:, v % 2, 0:n], spr_hi[:, sp_cols(v)].bitcast(F32),
                                            ALU.subtract).then_inc(sp_ready, 1)
                if u in (1, 6):
                    forget_gate(u // 6)
                for g in range(16, W_IN_PIECES):
                    if split_at(g) == u:
                        lo_early(g)
            dve.wait_ge(loga_ready, UNITS)
            chained(nc.vector.tensor_copy(c_hi, fu))
            nc.vector.tensor_tensor(c_lo, fu, c_hi.bitcast(F32), ALU.subtract).then_inc(c_split, 1)
            nc.vector.tensor_copy(sel8r, sel8).then_inc(c_split, 1)

            def stick_mix_lo(c):
                dve.wait_ge(mixs_hi, c + 1)
                nc.vector.scalar_tensor_tensor(out=hT_lo[:, 4 + c, :], in0=qk[:, 8 + c, :], scalar=gmix[:, 4 + c:5 + c],
                                               in1=hT_hi[:, 4 + c, :].bitcast(F32), op0=ALU.mult, op1=ALU.subtract).then_inc(mixs_lo, 1)

            def add_squares(kind, c, ready):
                dve.wait_ge(*ready)
                ins = nc.vector.tensor_tensor(qk[:, 12 * kind, :], qk[:, 12 * kind, :], qk[:, 12 * kind + c, :], ALU.add)
                if c < 3:
                    chained(ins)
                else:
                    ins.then_inc(sq_summed, 1)

            def mix_lo_part(n):
                half = slice(64 * (n % 2), 64 * (n % 2) + 64)
                c = n // 2
                dve.wait_ge(mix_sq, n + 1)
                nc.vector.scalar_tensor_tensor(out=hT_lo[half, c, :], in0=bank[3][half, :], scalar=gmix[half, c:c + 1],
                                               in1=hT_hi[half, c, :].bitcast(F32), op0=ALU.mult, op1=ALU.subtract).then_inc(mix_lo, 1)

            def add_oproj(half, j, b):
                t, h = j // 2, j % 2
                dve.wait_ge(oproj, 8 * half + j + 1)
                if half:
                    dve.wait_ge(x2_add, j + 1)
                dst = x2[t][:, h * BANK:(h + 1) * BANK]
                o = 0 if half else 4
                nc.vector.scalar_tensor_tensor(out=dst, in0=b[:], scalar=rm[:, o + t:o + t + 1], in1=dst,
                                               op0=ALU.mult, op1=ALU.add).then_inc(x2_add, 1)

            for u in range(UNITS + 4):
                if 3 <= u < UNITS + 3:
                    v = u - 3
                    n = (v % TT + 1) * P
                    dve.wait_ge(pt_turned, v + 1)
                    if v >= 2:
                        dve.wait_ge(pvf_done, v - 1)
                    nc.vector.tensor_copy(ptbuf[:, v % 2, 0:n], sbank[v % 4][:, 0:n]).then_inc(pt_ready, 1)
                if 1 <= u <= UNITS:
                    v = u - 1
                    n = (v % TT + 1) * P
                    dve.wait_ge(p_ready, v + 1)
                    chained(nc.vector.reciprocal(rinv[:, v % 2:v % 2 + 1], rsum[:, v % 2:v % 2 + 1]))
                    nc.vector.tensor_scalar(pbuf[:, v % 4, 0:n], pbuf[:, v % 4, 0:n], rinv[:, v % 2:v % 2 + 1], None,
                                            ALU.mult).then_inc(ps_ready, 1)
                if u < UNITS:
                    n = (u % TT + 1) * P
                    dve.wait_ge(s_ready, u + 1)
                    if u >= 2:
                        dve.wait_ge(neg_ready, u - 1)
                    chained(nc.vector.tensor_reduce(smax[:, u % 2:u % 2 + 1], sbank[u % 4][:, 0:n], AX.X, ALU.max))
                    if u >= 2:
                        dve.wait_ge(p_ready, u - 1)
                    nc.vector.tensor_scalar(negmax[:, u % 2:u % 2 + 1], smax[:, u % 2:u % 2 + 1], -1.0, None, ALU.mult).then_inc(neg_ready, 1)
                if u == 0:
                    v_evac(5)
                if 1 <= u < 5:
                    stick_mix_lo(u - 1)
                    if u >= 2:
                        add_squares(1, u - 1, (mixs_sq, u))
                    lo_early(W_IN_PIECES + u - 1)
                if u == 7:
                    dve.wait_ge(rsm_ready, 1)
                    dve.wait_ge(x2_in, 16 * TT)
                if u >= 9 and (u - 9) % 4 == 0:
                    add_oproj(0, (u - 9) // 4, bank[5 + (u - 9) // 4 % 3])
                if u >= 8 and (u - 8) % TT == 0:
                    n = (u - 8) // TT
                    mix_lo_part(n)
                    if n % 2 and n > 1:
                        add_squares(0, n // 2, (mix_sq, n + 1))
                if u > UNITS:
                    lo_early(W_IN_PIECES + 4 + u - UNITS - 1)
            add_squares(0, 3, (mix_sq, NH))
            mix_lo_part(NH - 1)
            add_oproj(0, 7, bank[5 + 7 % 3])
            lo_early(MOE0 - 1)
            dve.wait_ge(rsm_ready, 2)

            def normalise(t):
                dve.wait_ge(x2_rs, t + 1)
                nc.vector.reciprocal(r2[:, t:t + 1], rs2[:, t:t + 1]).then_inc(r2_ready, 1)
                dve.wait_ge(r2_ready, t + 1)
                nc.vector.scalar_tensor_tensor(out=tn[t], in0=x2[t], scalar=r2[:, t:t + 1], in1=g2b,
                                               op0=ALU.mult, op1=ALU.mult).then_inc(tn_ready, 1)

            for j in range(3):
                add_oproj(1, j, bank[j])
            dve.wait_ge(bias_hi, 2)
            nc.vector.tensor_tensor(bias1[32:64, :], b1raw[32:64, :], bias1[32:64, :].bitcast(F32), ALU.subtract).then_inc(bias_lo, 1)
            nc.vector.tensor_tensor(bias2[32:64, :], b2raw[32:64, :], bias2[32:64, :].bitcast(F32), ALU.subtract).then_inc(bias_lo, 1)
            add_oproj(1, 3, bank[3])
            dve.wait_ge(wrt_in, 32)
            nc.vector.tensor_tensor(wrg, wrt, g2col.unsqueeze(2).to_broadcast([P, KT, E]), ALU.mult).then_inc(wrg_ready, 1)
            dve.wait_ge(g2_in, 16)
            for j in range(4, 8):
                add_oproj(1, j, bank[j])
                if j % 2:
                    normalise(j // 2 - 2)
            normalise(2)
            normalise(3)

            def part(o, n):
                return rt[:, o:o + n]
            w4 = part(0, 16)
            v8 = part(16, 32)
            i8 = part(48, 32).bitcast(U32)
            kf = part(80, 16)
            lg = part(96, 128)
            oh = part(224, 512).rearrange("p (a e) -> p a e", e=E)
            pos = part(864, 128)
            cnt = part(992, 32)
            nov = part(1024, 32)
            incl = part(1056, 32)
            oba = part(1088, 32)
            jj = part(1120, 128)
            g1 = part(1248, 128)
            Bv = part(1376, 32)
            item = part(1408, 128)
            slt = part(1536, 128)
            sumw = part(1664, 4)
            item_k = part(1668, 16)
            slot_k = part(1684, 16)
            eidx = part(1700, ITEMS)
            tmp = part(1747, 47)
            tmp2 = part(1794, 47)
            dve.wait_ge(logits_done, 1)
            for t in range(TT):
                loose(nc.vector.scalar_tensor_tensor(out=lg[:, t * E:(t + 1) * E], in0=bank[1][:, t * E:(t + 1) * E],
                                                     scalar=r2[:, t:t + 1], in1=brb, op0=ALU.mult, op1=ALU.add))
            for t in range(TT):
                dve.wait_ge(steps["dve"], count["dve"] - TT + 1)
                loose(nc.vector.max(v8[:, 8 * t:8 * t + 8], lg[:, t * E:(t + 1) * E]))
            for t in range(TT):
                dve.wait_ge(steps["dve"], count["dve"] - TT + 1)
                loose(nc.vector.max_index(i8[:, 8 * t:8 * t + 8], v8[:, 8 * t:8 * t + 8], lg[:, t * E:(t + 1) * E]))
            v84 = v8.rearrange("p (t k) -> p t k", k=8)
            w44 = w4.rearrange("p (t k) -> p t k", k=TOPK)
            nc.vector.tensor_tensor(w44, v84[:, :, 0:4], v84[:, :, 0:1].to_broadcast([P, TT, TOPK]), ALU.subtract).then_inc(exp4, 1)
            dve.wait_ge(steps["dve"], count["dve"])
            chained(nc.vector.tensor_copy(kf.rearrange("p (t k) -> p t k", k=TOPK),
                                          i8.rearrange("p (t k) -> p t k", k=8)[:, :, 0:4]))
            iota_e = iotas[:, 0:E]
            chained(nc.vector.tensor_tensor(oh, iota_e.unsqueeze(1).to_broadcast([P, 16, E]),
                                            kf.unsqueeze(2).to_broadcast([P, 16, E]), ALU.is_equal))
            with nc.allow_low_precision(reason="the sum of at most one 1 and zeros is exact"):
                nc.vector.tensor_reduce(chosen.rearrange("p (t e) -> p t e", e=E),
                                        oh.rearrange("p (t k) e -> p t e k", k=TOPK), AX.X, ALU.add).then_inc(onehots, 1)
            dve.wait_ge(counted, 1)
            chained(nc.vector.tensor_copy(pos, bank[5][:, 0:128]))
            chained(nc.vector.tensor_copy(cnt, bank[5][:, 128:160]))
            chained(nc.vector.tensor_scalar(nov, cnt, float(P), None, ALU.is_gt))
            for j in (2, 3):
                chained(nc.vector.scalar_tensor_tensor(out=nov, in0=cnt, scalar=float(j * P), in1=nov, op0=ALU.is_gt, op1=ALU.add))
            chained(nc.vector.tensor_tensor_scan(incl, nov, ones[:, 0:E], 0.0, ALU.add, ALU.mult))
            chained(nc.vector.tensor_tensor(oba, incl, nov, ALU.subtract))
            chained(nc.vector.tensor_scalar(g1, pos, float(P), None, ALU.is_ge))
            chained(nc.vector.scalar_tensor_tensor(out=jj, in0=pos, scalar=2.0 * P, in1=g1, op0=ALU.is_ge, op1=ALU.add))
            chained(nc.vector.scalar_tensor_tensor(out=jj, in0=pos, scalar=3.0 * P, in1=jj, op0=ALU.is_ge, op1=ALU.add))
            chained(nc.vector.scalar_tensor_tensor(out=slt, in0=jj, scalar=-float(P), in1=pos, op0=ALU.mult, op1=ALU.add))
            chained(nc.vector.scalar_tensor_tensor(out=Bv, in0=oba, scalar=E - 1.0, in1=iota_e, op0=ALU.add, op1=ALU.subtract))
            i3 = item.rearrange("p (t e) -> p t e", e=E)
            chained(nc.vector.tensor_tensor(i3, g1.rearrange("p (t e) -> p t e", e=E), Bv.unsqueeze(1).to_broadcast([P, TT, E]), ALU.mult))
            chained(nc.vector.tensor_tensor(i3, i3, iota_e.unsqueeze(1).to_broadcast([P, TT, E]), ALU.add))
            chained(nc.vector.tensor_tensor(item, item, jj, ALU.add))
            pick = g2b[:, 0:512].rearrange("p (t k e) -> p t k e", t=TT, k=TOPK)
            oh4 = oh.rearrange("p (t k) e -> p t k e", k=TOPK)
            for src, dst in ((item, item_k), (slt, slot_k)):
                chained(nc.vector.tensor_tensor(pick, oh4, src.rearrange("p (t e) -> p t e", e=E).unsqueeze(2).to_broadcast([P, TT, TOPK, E]), ALU.mult))
                chained(nc.vector.tensor_reduce(dst.rearrange("p (t k) -> p t k", k=TOPK), pick, AX.X, ALU.add))
            dve.wait_ge(exp4, 2)
            chained(nc.vector.tensor_reduce(sumw, w44, AX.X, ALU.add))
            chained(nc.vector.reciprocal(sumw, sumw))
            chained(nc.vector.tensor_tensor(w44, w44, sumw.unsqueeze(2).to_broadcast([P, TT, TOPK]), ALU.mult))
            dve.wait_ge(tn_out, 16 * TT)
            for a in range(0, 16, 8):
                h = slice(a, a + 8)
                loose(nc.vector.tensor_tensor(ohslot[:, h], iotas[:].unsqueeze(1).to_broadcast([P, 8, P]),
                                              slot_k[:, h].unsqueeze(2).to_broadcast([P, 8, P]), ALU.is_equal))
                chained(nc.vector.tensor_tensor(payload[:, h, 1, :], iotas[:, 0:ITEMS].unsqueeze(1).to_broadcast([P, 8, ITEMS]),
                                                item_k[:, h].unsqueeze(2).to_broadcast([P, 8, ITEMS]), ALU.is_equal))
                chained(nc.vector.tensor_tensor(payload[:, h, 0, :], payload[:, h, 1, :],
                                                row1[:, h].unsqueeze(2).to_broadcast([P, 8, ITEMS]), ALU.mult))
                nc.vector.tensor_tensor(payload[:, h, 1, :], payload[:, h, 1, :],
                                        w4[:, h].unsqueeze(2).to_broadcast([P, 8, ITEMS]), ALU.mult).then_inc(slots_ready, 1)
            chained(nc.vector.tensor_copy(eidx[:, 0:E], iota_e))
            ra = oh.rearrange("p a e -> p (a e)")[:, 0:OVER * E].rearrange("p (i e) -> p i e", e=E)
            rb = pick.rearrange("p t k e -> p (t k e)")[:, 0:OVER * E].rearrange("p (i e) -> p i e", e=E)
            io = iotas[:, 0:OVER].unsqueeze(2).to_broadcast([P, OVER, E])
            chained(nc.vector.tensor_tensor(ra, io, oba.unsqueeze(1).to_broadcast([P, OVER, E]), ALU.is_ge))
            chained(nc.vector.tensor_tensor(rb, io, incl.unsqueeze(1).to_broadcast([P, OVER, E]), ALU.is_lt))
            chained(nc.vector.tensor_tensor(ra, ra, rb, ALU.mult))
            chained(nc.vector.tensor_tensor(ra, ra, iota_e.unsqueeze(1).to_broadcast([P, OVER, E]), ALU.mult))
            chained(nc.vector.tensor_reduce(eidx[:, E:ITEMS], ra, AX.X, ALU.add))
            chained(nc.vector.tensor_copy(eidtab[0:1, 0:OVER], eidx[0:1, E:ITEMS]))
            chained(nc.vector.tensor_copy(novi[:], incl[0:1, E - 1:E]))
            chained(nc.vector.tensor_scalar(seltab[:], eidx[0:64, :], pmod, None, ALU.is_equal))
            dve.wait_ge(tab_mm, 1)
            chained(nc.vector.tensor_copy(wtab[:], bank[5][:, 256 + ITEMS:256 + 2 * ITEMS]))
            chained(nc.vector.tensor_scalar(tmp, bank[5][:, 256:256 + ITEMS], 0.0, EMPTY, ALU.is_equal, ALU.mult))
            chained(nc.vector.scalar_tensor_tensor(out=tmp2, in0=bank[5][:, 256:256 + ITEMS], scalar=-1.0, in1=tmp,
                                                   op0=ALU.add, op1=ALU.add))
            chained(nc.vector.tensor_copy(stab[:], tmp2))
            nc.vector.tensor_scalar(gtab[:], stab[:], 2, None, ALU.arith_shift_right).then_inc(tables, 1)

            def lo_moe(j, z, at):
                h = j % 2
                lo(stage_lo[:, j % STAGES, :], slot(z)[:, h * PIECE:(h + 1) * PIECE], stage_hi[:, j % STAGES, :], at)

            def turned_lo(dst_lo, dst_hi, ready, done, t, tiles):
                for h in range(2):
                    n = min(tiles - 4 * h, 4)
                    dve.wait_ge(ready, t * 2 + (h + 1))
                    nc.vector.tensor_tensor(dst_lo[:, 4 * h:4 * h + n, :], bank[6 + h][:, 0:n * P].rearrange("p (k t) -> p k t", k=n),
                                            dst_hi[:, 4 * h:4 * h + n, :].bitcast(F32), ALU.subtract).then_inc(done, 1)

            def at_col(tab, i, rows=P):
                return tab[0:rows, i:i + 1] if isinstance(i, int) else tab[0:rows, bass.ds(i, 1)]

            def select1(i):
                wait(dve, sel1_used, i)
                nc.vector.tensor_copy(sel1, at_col(seltab, i, 64).to_broadcast([64, P])).then_inc(sel1_r, 1)

            def select2(i, used_at):
                dve.wait_ge(used, used_at)
                nc.vector.tensor_copy(sel2, at_col(seltab, i, 64).to_broadcast([64, P])).then_inc(sel2_r, 1)

            def weights(i):
                wait(dve, y_ready, i)
                nc.vector.tensor_copy(wcol[:], at_col(wtab, i)).then_inc(weight_ready, 1)

            def clip(t, part_, used_at):
                if part_ == 0:
                    dve.wait_ge(used, used_at)
                    wait(dve, act_made, t)
                    for h in range(2):
                        ins = nc.vector.tensor_scalar(glu[:, h * BANK:(h + 1) * BANK], bank[h][:], LIMIT, None, ALU.min)
                else:
                    wait(dve, a_turned, t)
                    for h in range(2):
                        ins = nc.vector.tensor_scalar(lin[:, h * BANK:(h + 1) * BANK], bank[2 + h][:], LIMIT, -LIMIT,
                                                      ALU.min, ALU.max)
                ins.then_inc(clipped, 1)

            def gated(t):
                dve.wait_ge(sig_done, t + 1)
                nc.vector.tensor_tensor(sig, sig, glu, ALU.mult).then_inc(gs_made, 1)
                dve.wait_ge(gs_made, t + 1)
                dve.wait_ge(clipped, t * 2 + 2)
                nc.vector.scalar_tensor_tensor(out=lin, in0=lin, scalar=1.0, in1=sig, op0=ALU.add, op1=ALU.mult).then_inc(act_made, 1)

            def run_items(run):
                q0, n, b = run.first, run.n, run.base
                ub = b - OPROJ_PIECES
                select1(q0)
                for j in range(W1P):
                    if j == STAGES:
                        turned_lo(xT_lo, xT_hi, xT_hi_r, xT_lo_r, q0, KT - 1)
                    if j < WHOLE:
                        lo_moe(j, moe_slot(j // 2), run.split0 + j + 1)
                    if j == 2:
                        select2(q0, ub)
                        weights(q0)
                    if j == 4:
                        select1(q0 + 1)
                clip(q0, 0, ub + W1P)
                clip(q0, 1, ub + W1P)
                turned_lo(xT_lo, xT_hi, xT_hi_r, xT_lo_r, q0 + 1, KT - 1)

                def body(r, first=False, last=False):
                    t = r + q0
                    for j in range(W1P + W2P):
                        if j not in (WHOLE, WHOLE + 1):
                            lo_moe(j, (j // 2 + 8) % SLOTS, run.split(r, j))
                        if j == 1:
                            gated(t - 1)
                        if j == 5 and not first:
                            select2(t - 1, r * 24 + (ub - 8))
                            weights(t - 1)
                        if j == 7 and not last:
                            select1(t + 1)
                        if j == 12:
                            turned_lo(aT_lo, aT_hi, aT_hi_r, aT_lo_r, t - 1, KT)
                        if j == 17:
                            clip(t, 0, r * 24 + (ub - 8 + W1P))
                        if j == 18:
                            clip(t, 1, None)
                        if j == 21 and not last:
                            turned_lo(xT_lo, xT_hi, xT_hi_r, xT_lo_r, t + 1, KT - 1)
                body(1, first=True)
                with dve.Fori(2, n - 1) as r:
                    body(r)
                body(n - 1, last=True)
                gated(q0 + n - 1)
                turned_lo(aT_lo, aT_hi, aT_hi_r, aT_lo_r, q0 + n - 1, KT)
                for j in range(W2P):
                    c = (24 * n - 8) // 2 + j // 2
                    lo_moe(j, moe_slot(c), run.split(n, j))
                    if j == 0:
                        select2(q0 + n - 1, ub + 24 * n - 8)
                        weights(q0 + n - 1)

            run_items(MAIN)
            n_over = dve.value_load(novi[0:1, 0:1], min_val=0, max_val=OVER)
            with dve.If(n_over > 0):
                run_items(REST)
                dve.wait_ge(fin_again, 16 * TT)

            dve.wait_ge(gf_in, 16)
            def final(t):
                acc = ring[:, t * 5 * D:t * 5 * D + D]
                dve.wait_ge(fin_rs, t + 1)
                chained(nc.vector.reciprocal(r3[:, t:t + 1], rs3[:, t:t + 1]))
                nc.vector.scalar_tensor_tensor(out=acc, in0=acc, scalar=r3[:, t:t + 1], in1=gfb, op0=ALU.mult,
                                               op1=ALU.mult).then_inc(fin_ready, 1)
            for t in range(TT):
                o = t * 5 * D
                acc = ring[:, o:o + D]
                for j in range(TOPK):
                    if j == 0:
                        dve.wait_ge(fin_in[t][0], 16)
                    dve.wait_ge(fin_in[t][j + 1], 16)
                    nc.vector.tensor_tensor(acc, acc, ring[:, o + (j + 1) * D:o + (j + 2) * D], ALU.add).then_inc(fin_sum, 1)
                    dve.wait_ge(fin_sum, 4 * t + j + 1)
                if t >= 1:
                    final(t - 1)
            final(TT - 1)

        @block.tensor
        def _(pe):
            def three(dst, w_hi, w_lo, m_hi, m_lo, start, stop):
                pe.matmul(dst, w_hi, m_hi, start=start, stop=False)
                pe.matmul(dst, w_hi, m_lo, start=False, stop=False)
                return pe.matmul(dst, w_lo, m_hi, start=False, stop=stop)

            pe.wait_ge(consts, 1)
            for j in range(2 * TT):
                t, h = j // 2, j % 2
                pe.wait_ge(h_norm, t + 1)
                if j >= 4:
                    pe.wait_ge(h_lo, j - 3)
                for k in range(4):
                    mm = pe.transpose(bank[4 + j % 4][:, k * P:(k + 1) * P], xs[t][:, (4 * h + k) * P:(4 * h + k + 1) * P], identF[:])
                mm.then_inc(h_turned, 1)
            pe.wait_ge(h_lo, 2 * TT)

            def project(g, kk, c):
                group, k = g // 4, 2 * (g % 4) + kk
                b = bank[c if group in (0, 2) else 4 + c]
                if kk == 0 and c == 0:
                    pe.wait_ge(split_lo, g + 1)
                if k == 0 and group >= 2:
                    pe.wait_ge(qk_copied, {2: 0, 3: 4, 4: 8, 5: 12}[group] + c + 1)
                whi = stage_hi[:, g % STAGES, kk * BANK:(kk + 1) * BANK]
                wlo = stage_lo[:, g % STAGES, kk * BANK:(kk + 1) * BANK]
                cs = slice(c * P, (c + 1) * P)
                if group in (2, 5):
                    mm = three(b[:], hT_hi[:, k, cs], hT_lo[:, k, cs], whi, wlo, k == 0, k == KT - 1)
                else:
                    mm = three(b[:], whi[:, cs], wlo[:, cs], hT_hi[:, k, :], hT_lo[:, k, :], k == 0, k == KT - 1)
                if kk == 1 and c == 3:
                    mm.then_inc(used, 1)

            for g in range(12):
                for kk in range(2):
                    for c in range(4):
                        project(g, kk, c)

            def forget_logits(k0):
                if k0 == 0:
                    pe.wait_ge(f_split, 2)
                    pe.wait_ge(v_copied, TT)
                for k in range(k0, k0 + 4):
                    fs = slice(k * NH, (k + 1) * NH)
                    mm = three(bank[3][0:NH, :], wfr[:, 0, fs], wfr[:, 1, fs], hT_hi[:, k, :], hT_lo[:, k, :], k == 0, k == KT - 1)
                if k0:
                    mm.then_inc(f_mm, 1)

            def scores(u):
                n, i = u // TT, u % TT
                half = slice(64 * (n % 2), 64 * (n % 2) + 64)
                b = sbank[u % 4]
                dst = b[:, 0:(i + 1) * P]
                if u >= 4:
                    pe.wait_ge(pt_ready, u - 3)
                pe.matmul(b[:, i * P:(i + 1) * P], identB[:], maskF, start=True, stop=False, skip_group_check=True)
                pe.matmul(dst, qk[half, n // 2, i * P:(i + 1) * P], qk[half, 4 + n // 2, 0:(i + 1) * P], start=False,
                          stop=False, skip_group_check=True)
                pe.matmul(dst, sel8r[:, n, :], c_hi[:, 0:(i + 1) * P], start=False, stop=False, skip_group_check=True)
                pe.matmul(dst, sel8r[:, n, :], c_lo[:, 0:(i + 1) * P], start=False, stop=True,
                          skip_group_check=True).then_inc(s_ready, 1)

            def z_scores(u):
                n, j = u // TT, TT - 1 - u % TT
                half = slice(64 * (n % 2), 64 * (n % 2) + 64)
                b = bank[u % 3]
                if u >= 3:
                    pe.wait_ge(a_ready, u - 2)
                else:
                    pe.wait_ge(v_copied, u + 1)
                pe.matmul(b[:, 0:P], identB[:], maskS, start=True, stop=False, skip_group_check=True)
                pe.matmul(b[:, 0:S - j * P], qk[half, 12 + n // 2, j * P:(j + 1) * P], qk[half, 8 + n // 2, j * P:S],
                          start=False, stop=True, skip_group_check=True).then_inc(z_ready, 1)

            def turn_p(u):
                pe.wait_ge(ps_ready, u + 1)
                for kb in range(u % TT + 1):
                    mm = pe.transpose(sbank[u % 4][:, kb * P:(kb + 1) * P], pbuf[:, u % 4, kb * P:(kb + 1) * P], identF[:])
                mm.then_inc(pt_turned, 1)

            def log_a(u):
                i = u % TT
                b = bank[u % 3]
                pe.wait_ge(sp_ready, u + 1)
                if u == 0:
                    pe.wait_ge(tri_ready, 2)
                for v in range(u - i, u + 1):
                    o = P * (v % TT) * (v % TT + 1) // 2
                    w = P * (v % TT + 1)
                    for part in (spr_hi, spr_lo):
                        mm = pe.matmul(b[:, (i + 1) * P - w:(i + 1) * P], (neg_tri if v == u else neg_one)[:], part[:, o:o + w],
                                       start=False, stop=v == u and part is spr_lo, skip_group_check=True)
                mm.then_inc(loga_ready, 1)

            def pv_fox(u):
                n, i = u // TT, u % TT
                half = slice(64 * (n % 2), 64 * (n % 2) + 64)
                pe.wait_ge(pt_ready, u + 1)
                if i == 0 and n >= 2:
                    pe.wait_ge(mix_lo, n - 1)
                for kb in range(i + 1):
                    mm = pe.matmul(bank[3][half, i * P:(i + 1) * P], vbuf[:, kb, n * HD:(n + 1) * HD],
                                   ptbuf[:, u % 2, kb * P:(kb + 1) * P], start=kb == 0, stop=kb == i)
                mm.then_inc(pvf_done, 1)

            def pv_stick(u):
                n, i = u // TT, u % TT
                j = TT - 1 - i
                half = slice(64 * (n % 2), 64 * (n % 2) + 64)
                pe.wait_ge(a_ready, u + 1)
                if i == 0 and n >= 2:
                    pe.wait_ge(o_copied, n - 1)
                if u == 0:
                    pe.wait_ge(f_steps, 1)
                pe.matmul(bank[3][half, j * P:S], vbuf[:, j, HW + n * HD:HW + (n + 1) * HD], abuf[:, u % 2, 0:(i + 1) * P],
                          start=i == 0, stop=i == TT - 1, skip_group_check=True).then_inc(pvs_done, 1)

            pe.wait_ge(qk_copied, 8)
            pe.wait_ge(consts, 15)
            fill = [(g, kk, c) for g in range(12, W_IN_PIECES) for kk in range(2) for c in range(4)]
            for u in range(UNITS + 3):
                if u < UNITS:
                    z_scores(u)
                if u < FILL0:
                    forget_logits(4 * u)
                for part in range(3):
                    if part == 1 and 2 <= u < UNITS + 2:
                        log_a(u - 2)
                    if part == 2 and u >= 3:
                        pv_stick(u - 3)
                    if FILL0 <= u < FILL0 + UNITS:
                        project(*fill[3 * (u - FILL0) + part])

            def sums(kind):
                pe.wait_ge(sq_summed, 2 - kind)
                for t in range(TT):
                    mm = pe.matmul(bank[7][:, 4 * kind + t:4 * kind + t + 1], qk[:, 12 * kind, t * P:(t + 1) * P],
                                   ones[:, 0:1], start=True, stop=True)
                mm.then_inc(ssm_done, 1)

            def out_project(half, i, j, b):
                t, h = j // 2, j % 2
                c = 4 - 4 * half + i
                ts = slice(t * P, (t + 1) * P)
                hs = slice(h * BANK, (h + 1) * BANK)
                return three(b[:], hT_hi[:, c, ts], hT_lo[:, c, ts], stage_hi[:, i, hs], stage_lo[:, i, hs], i == 0, i == 3)

            pe.wait_ge(c_split, 2)
            pe.wait_ge(qk_copied, 16)
            for u in range(UNITS + 4):
                if 3 <= u < UNITS + 3:
                    turn_p(u - 3)
                if u >= 4:
                    if u == 4:
                        pe.wait_ge(v_copied, 2 * TT)
                        pe.wait_ge(o_copied, NH)
                    if u < 8:
                        pe.wait_ge(mixs_lo, u - 3)
                        pe.wait_ge(split_lo, W_IN_PIECES + u - 3)
                    if u == 6:
                        sums(1)
                    pv_fox(u - 4)
                    j, i = (u - 4) // 4, (u - 4) % 4
                    if i == 0 and j == 2:
                        pe.wait_ge(ms_read, 1)
                    if i == 0 and j >= 3:
                        pe.wait_ge(x2_add, j - 2)
                    mm = out_project(0, i, j, bank[5 + j % 3])
                    if j == 7 and i < 3:
                        mm.then_inc(stage_left, 1)
                    if i == 3:
                        mm.then_inc(oproj, 1)
                if u < UNITS:
                    scores(u)
            def fox_block(j, pieces=range(4)):
                for i in pieces:
                    pe.wait_ge(split_lo, W_IN_PIECES + 4 + i + 1)
                    mm = out_project(1, i, j, bank[j])
                    if i == 3:
                        mm.then_inc(oproj, 1)

            def turn_x2(j):
                pe.wait_ge(x2_add, 2 * TT + j + 1)
                t, h = j // 2, j % 2
                for k in range(4):
                    mm = pe.transpose(bank[j][:, k * P:(k + 1) * P], x2[t][:, (4 * h + k) * P:(4 * h + k + 1) * P], identF[:])
                mm.then_inc(x2_turned, 1)

            def logits(t):
                pe.wait_ge(tT_copied, 2 * t + 2)
                if t == 0:
                    pe.wait_ge(wrg_ready, 1)
                else:
                    pe.wait_ge(lgT_copied, t)
                for k in range(KT):
                    mm = pe.matmul(bank[0][0:E, t * P:(t + 1) * P], wrg[:, k, :], tT[k // 4][:, k % 4, t * P:(t + 1) * P],
                                   start=k == 0, stop=k == KT - 1)
                mm.then_inc(lgT_done, 1)

            pe.wait_ge(mix_lo, 6)
            for i in range(3):
                for j in range(3):
                    fox_block(j, (i,))
            pe.wait_ge(x2_add, 8)
            sums(0)
            pe.wait_ge(mix_lo, NH)
            for j in range(3):
                fox_block(j, (3,))
            fox_block(3)
            fox_block(4)
            turn_x2(0)
            fox_block(5)
            turn_x2(1)
            fox_block(6)
            logits(0)
            turn_x2(2)
            turn_x2(3)
            pe.wait_ge(ms_read, 2)
            fox_block(7)
            logits(1)
            turn_x2(4)
            turn_x2(5)
            logits(2)
            turn_x2(6)
            turn_x2(7)
            logits(3)
            pe.wait_ge(lgT_copied, TT)
            for t in range(TT):
                mm = pe.transpose(bank[1][:, t * E:(t + 1) * E], lgT[:, t * P:(t + 1) * P], identF[0:E, 0:E])
            mm.then_inc(logits_done, 1)
            pe.wait_ge(onehots, 1)
            for t in range(TT):
                for v in range(t + 1):
                    pe.matmul(bank[5][:, t * E:(t + 1) * E], (before if v == t else onesB)[:], chosen[:, v * E:(v + 1) * E],
                              start=v == 0, stop=v == t)
            for v in range(TT):
                mm = pe.matmul(bank[5][:, 128:160], onesB[:], chosen[:, v * E:(v + 1) * E], start=v == 0, stop=v == TT - 1)
            mm.then_inc(counted, 1)
            for a in range(16):
                if a % 8 == 0:
                    pe.wait_ge(slots_ready, a // 8 + 1)
                mm = pe.matmul(bank[5][:, 256:256 + 2 * ITEMS], ohslot[:, a, :], payload[:, a].rearrange("p c n -> p (c n)"),
                               start=a == 0, stop=a == 15)
            mm.then_inc(tab_mm, 1)

            def turn_x(t):
                pe.wait_ge(gathered, t * 16 + 16)
                for k in range(KT):
                    mm = pe.transpose(bank[6 + k // 4][:, k % 4 * P:(k % 4 + 1) * P], gath[:, k * P:(k + 1) * P], identF[:])
                mm.then_inc(x_turned, 1)

            def turn_a(t):
                pe.wait_ge(act_made, t + 1)
                for k in range(KT):
                    mm = pe.transpose(bank[6 + k // 4][:, k % 4 * P:(k % 4 + 1) * P], lin[:, k * P:(k + 1) * P], identF[:])
                mm.then_inc(a_turned, 1)

            def bias_1(t):
                pe.wait_ge(sel1_r, t + 1)
                wait(pe, clipped, t * 2)
                for c in range(4):
                    mm = pe.matmul(bank[c][:], sel1, bias1[:, c * BANK:(c + 1) * BANK], start=True, stop=False)
                mm.then_inc(sel1_used, 1)

            def bias_2(t):
                pe.wait_ge(sel2_r, t + 1)
                wait(pe, y_ready, t)
                for c in range(2):
                    pe.matmul(bank[4 + c][:], sel2, bias2[:, c * BANK:(c + 1) * BANK], start=True, stop=False)

            def multiply(j, at, T_hi, T_lo, k, b0, stop):
                pe.wait_ge(split_lo, at)
                for (w, m) in ((T_hi, stage_hi), (T_hi, stage_lo), (T_lo, stage_hi)):
                    for h in range(2):
                        mm = pe.matmul(bank[b0 + h][:], w[:, k, :], m[:, j % STAGES, h * BANK:(h + 1) * BANK],
                                       start=False, stop=stop and w is T_lo)
                mm.then_inc(used, 1)

            def multiply_whole(j, z, turns):
                if j == WHOLE:
                    pe.wait_ge(full[z], turns)
                for h in range(2):
                    mm = pe.matmul(bank[2 * (j % 2) + h][:], xT_7, slot(z)[:, j % 2 * PIECE + h * BANK:j % 2 * PIECE + (h + 1) * BANK],
                                   start=False, stop=True)
                mm.then_inc(used, 1)

            def run_items(run):
                q0, n, b, T0 = run.first, run.n, run.base, run.turn0
                zf, zb = moe_slot(KT - 1), (KT - 1 + 8) % SLOTS
                bias_1(q0)
                turn_x(q0)
                pe.wait_ge(xT_lo_r, 2 * q0 + 2)
                for j in range(WHOLE):
                    multiply(j, run.split0 + j + 1, xT_hi, xT_lo, j // 2, 2 * (j % 2), False)
                for j in (WHOLE, WHOLE + 1):
                    multiply_whole(j, zf, 16 * (loads_before(zf) + T0 + 1))
                turn_x(q0 + 1)

                def body(r, last=False):
                    t = r + q0
                    bias_1(t)
                    pe.wait_ge(xT_lo_r, t * 2 + 2)
                    for j in range(W1P):
                        if j < WHOLE:
                            multiply(j, run.split(r, j), xT_hi, xT_lo, j // 2, 2 * (j % 2), False)
                        else:
                            multiply_whole(j, zb, r * 16 + 16 * (loads_before(zb) + T0 + 1))
                        if j == 8:
                            turn_a(t - 1)
                    pe.wait_ge(aT_lo_r, t * 2)
                    if not last:
                        turn_x(t + 1)
                    bias_2(t - 1)
                    for j in range(W2P):
                        multiply(j, run.split(r, W1P + j), aT_hi, aT_lo, j, 4, j == KT - 1)
                body(1)
                with pe.Fori(2, n - 1) as r:
                    body(r)
                body(n - 1, last=True)
                turn_a(q0 + n - 1)
                pe.wait_ge(aT_lo_r, 2 * (q0 + n))
                bias_2(q0 + n - 1)
                for j in range(W2P):
                    multiply(j, run.split(n, j), aT_hi, aT_lo, j, 4, j == KT - 1)

            pe.wait_ge(bias_lo, 2)
            run_items(MAIN)
            pe.wait_ge(tables, 1)
            n_over = pe.value_load(novi[0:1, 0:1], min_val=0, max_val=OVER)
            with pe.If(n_over > 0):
                run_items(REST)


_INS = ["x", "norm1_g", "w_in", "b_f", "g_fox", "g_sb", "w_out", "norm2_g", "w_router", "b_router",
        "w1", "b1", "w2", "b2", "norm_f_g"]


def kernel(**inputs):
    import numpy as np
    import concourse.bacc as bacc
    from concourse.bass_utils import run_bass_kernel_spmd

    nc = bacc.Bacc("TRN2", target_bir_lowering=False, num_devices=1)
    arrays, args = {}, []
    for name in _INS:
        a = np.ascontiguousarray(inputs[name])
        arrays[f"in_{name}"] = a
        args.append(nc.dram_tensor(f"in_{name}", a.shape, mybir.dt.from_np(a.dtype), kind="ExternalInput").ap())
    out = nc.dram_tensor("out", (1, S, D), F32, kind="ExternalOutput").ap()
    build(nc, *args, out)
    r = run_bass_kernel_spmd(nc, [arrays], core_ids=[0])
    return r.results[0]["out"]
```
